# Optimizing a Trainium2 kernel written in Bass

```python
import jax, jax.numpy as jnp
from jax import lax
import numpy as np

D_MODEL = 2048
BATCH = 1
SEQ = 256
DEPTH = 2

N_A = DEPTH // 2
N_B = DEPTH - N_A
CHUNK = 128
D_A = D_MODEL
G_A = 16
GD_A = D_A // G_A
N_HEADS = 16
HEAD_DIM = 128
D_B = N_HEADS * HEAD_DIM
BLOCK_Q = 128
D_FF = 5632
CONV_W = 3
EPS = 1e-6

kernel_name = "yoco_gmlp_stickbreaking_hybrid"

def rms_norm(x, g):
    xf = x.astype(jnp.float32)
    ms = jnp.mean(xf * xf, axis=-1, keepdims=True)
    return (xf * lax.rsqrt(ms + EPS) * g.astype(jnp.float32)).astype(x.dtype)

def chunked_gmlp(h, w_in, v_g, w_s, b_s, w_out):
    B, S, _ = h.shape
    uv = jax.nn.gelu(h @ w_in)
    u, v = jnp.split(uv, 2, axis=-1)
    v = rms_norm(v.reshape(B, S, G_A, GD_A), v_g.reshape(G_A, GD_A))
    v = v.reshape(B, S // CHUNK, CHUNK, G_A, GD_A)
    causal = jnp.tril(jnp.ones((CHUNK, CHUNK), dtype=w_s.dtype))
    w = w_s * causal[None]
    mixed = jnp.einsum('gts,bnsgd->bntgd', w, v) + b_s.T[None, None, :, :, None]
    out = u * mixed.reshape(B, S, D_A)
    return out @ w_out

def stick_breaking_attention(q, k, v):
    B, S, H, dh = q.shape
    nb = S // BLOCK_Q
    scale = 1.0 / np.sqrt(dh).astype(np.float32)
    qb = q.reshape(B, nb, BLOCK_Q, H, dh).transpose(1, 0, 2, 3, 4)
    kf = k.astype(jnp.float32)
    vf = v.astype(jnp.float32)
    kpos = jnp.arange(S)

    def one_block(args):
        qi, i = args
        z = jnp.einsum('bqhd,bkhd->bhqk', qi.astype(jnp.float32), kf) * scale
        qpos = i * BLOCK_Q + jnp.arange(BLOCK_Q)
        mask = kpos[None, :] < qpos[:, None]
        log_beta = jax.nn.log_sigmoid(z)
        log_1m = jnp.where(mask, jax.nn.log_sigmoid(-z), 0.0)
        suffix = jnp.flip(jnp.cumsum(jnp.flip(log_1m, -1), axis=-1), -1) - log_1m
        a = jnp.where(mask, jnp.exp(log_beta + suffix), 0.0)
        return jnp.einsum('bhqk,bkhd->bqhd', a, vf)

    out = lax.map(one_block, (qb, jnp.arange(nb)))
    return out.transpose(1, 0, 2, 3, 4).reshape(B, S, H * dh).astype(q.dtype)

def conv_ffn(h, w_up, conv_w, conv_b, w_down):
    S = h.shape[1]
    a = h @ w_up
    ap = jnp.pad(a, ((0, 0), (CONV_W - 1, 0), (0, 0)))
    c = conv_b + sum(ap[:, tap:tap + S] * conv_w[tap] for tap in range(CONV_W))
    gate, val = jnp.split(c, 2, axis=-1)
    return (jax.nn.silu(gate) * val) @ w_down

def setup_inputs(seed: int = 0) -> dict:
    key = jax.random.key(seed)
    ks = jax.random.split(key, 24)
    f32 = jnp.float32

    def nrm(k, shape, scale):
        return jax.random.normal(k, shape, f32) * scale

    def gain(k, shape):
        return 1.0 + 0.02 * jax.random.normal(k, shape, f32)

    return {
        "x": jax.random.normal(ks[0], (BATCH, SEQ, D_MODEL), f32),
        "pre_mix_g": gain(ks[1], (DEPTH, D_MODEL)),
        "post_mix_g": gain(ks[2], (DEPTH, D_MODEL)),
        "pre_ffn_g": gain(ks[3], (DEPTH, D_MODEL)),
        "post_ffn_g": gain(ks[4], (DEPTH, D_MODEL)),
        "a_w_in": nrm(ks[5], (N_A, D_MODEL, 2 * D_A), D_MODEL ** -0.5),
        "a_v_norm_g": gain(ks[6], (N_A, D_A)),
        "a_w_spatial": nrm(ks[7], (N_A, G_A, CHUNK, CHUNK), CHUNK ** -0.5),
        "a_b_spatial": gain(ks[8], (N_A, G_A, CHUNK)),
        "a_w_out": nrm(ks[9], (N_A, D_A, D_MODEL), D_A ** -0.5),
        "kv_norm_g": gain(ks[10], (D_MODEL,)),
        "w_k": nrm(ks[11], (D_MODEL, D_B), D_MODEL ** -0.5),
        "w_v": nrm(ks[12], (D_MODEL, D_B), D_MODEL ** -0.5),
        "b_w_q": nrm(ks[13], (N_B, D_MODEL, D_B), D_MODEL ** -0.5),
        "b_w_o": nrm(ks[14], (N_B, D_B, D_MODEL), D_B ** -0.5),
        "ffn_w_up": nrm(ks[15], (DEPTH, D_MODEL, 2 * D_FF), D_MODEL ** -0.5),
        "ffn_conv_w": nrm(ks[16], (DEPTH, CONV_W, 2 * D_FF), CONV_W ** -0.5),
        "ffn_conv_b": nrm(ks[17], (DEPTH, 2 * D_FF), 0.02),
        "ffn_w_down": nrm(ks[18], (DEPTH, D_FF, D_MODEL), D_FF ** -0.5),
    }

def reference(x, pre_mix_g, post_mix_g, pre_ffn_g, post_ffn_g,
              a_w_in, a_v_norm_g, a_w_spatial, a_b_spatial, a_w_out,
              kv_norm_g, w_k, w_v, b_w_q, b_w_o,
              ffn_w_up, ffn_conv_w, ffn_conv_b, ffn_w_down):
    B, S, _ = x.shape
    h = x
    k_shared = None
    v_shared = None
    for layer in range(DEPTH):
        hn = rms_norm(h, pre_mix_g[layer])
        if layer < N_A:
            mix = chunked_gmlp(hn, a_w_in[layer], a_v_norm_g[layer],
                               a_w_spatial[layer], a_b_spatial[layer], a_w_out[layer])
        else:
            j = layer - N_A
            if j == 0:
                kvn = rms_norm(h, kv_norm_g)
                k_shared = (kvn @ w_k).reshape(B, S, N_HEADS, HEAD_DIM)
                v_shared = (kvn @ w_v).reshape(B, S, N_HEADS, HEAD_DIM)
            q = (hn @ b_w_q[j]).reshape(B, S, N_HEADS, HEAD_DIM)
            mix = stick_breaking_attention(q, k_shared, v_shared) @ b_w_o[j]
        h = h + rms_norm(mix, post_mix_g[layer])
        f = conv_ffn(rms_norm(h, pre_ffn_g[layer]), ffn_w_up[layer],
                     ffn_conv_w[layer], ffn_conv_b[layer], ffn_w_down[layer])
        h = h + rms_norm(f, post_ffn_g[layer])
    return h


_drawn_inputs = setup_inputs


def setup_inputs(seed=0):
    import zlib

    import numpy as np

    out = dict(_drawn_inputs(seed))
    spreads = {}
    factors = {'post_ffn_g': 3.572, 'a_v_norm_g': 16.501, 'a_b_spatial': 11.111, 'kv_norm_g': 86.701}
    for name, (base, spread) in spreads.items():
        noise = np.random.default_rng([zlib.crc32(name.encode()), seed]).standard_normal(out[name].shape)
        drawn = base * np.exp(spread * noise) if base else spread * noise
        out[name] = __import__('jax').numpy.asarray(drawn.astype(out[name].dtype))
    for name, factor in factors.items():
        out[name] = (out[name] * factor).astype(out[name].dtype)
    return out
```

```python
from contextlib import ExitStack

import concourse.bass as bass
from concourse import mybir

ALU = mybir.AluOpType
ACT = mybir.ActivationFunctionType
AX = mybir.AxisListType
F32 = mybir.dt.float32
F32R = mybir.dt.float32r

P = 128
BLK = 512
UK = 2
RING = 4
EPS = 1e-6
HI, LO = 0, 1
SBUF_START = 16512


class Phase:

    def __init__(self, before, w, starts, step, pairs):
        self.w, self.starts, self.step, self.pairs = w, starts, step, pairs
        self.units = w.shape[0] // (UK * P)
        self.first = before.end if before else 0
        self.block0 = before.block_end if before else 0
        self.end = self.first + 2 * pairs * self.units
        self.block_end = self.block0 + 2 * pairs

    def column(self, i, h):
        return self.starts[h] + i * self.step

    def unit(self, b):
        return self.first + b * self.units


def build_trunk(nc, x, pre_mix_g, post_mix_g, pre_ffn_g, post_ffn_g, a_w_in, a_v_norm_g, a_w_spatial,
                a_b_spatial, a_w_out, kv_norm_g, w_k, w_v, b_w_q, b_w_o, ffn_w_up, ffn_conv_w,
                ffn_conv_b, ffn_w_down, out):
    _, T, D = x.shape
    NH = T // P
    KT = D // P
    G = a_w_spatial.shape[1]
    FF = ffn_w_down.shape[1]
    FT = FF // P
    HEADS = w_k.shape[1] // P
    NB = D // BLK
    TB = BLK // P
    FP = FF // BLK
    TAPS = ffn_conv_w.shape[1]
    PAD = TAPS - 1
    ATT = T + P
    STEPS = HEADS // 2
    LAST = NB - 1
    SCALE = float(P) ** -0.5
    assert T == 2 * P and G == KT and HEADS == KT and a_w_spatial.shape[2] == P

    gate_v = Phase(None, a_w_in[0], (D, D + BLK), 2 * BLK, NB // 2)
    gate_u = Phase(gate_v, a_w_in[0], (0, BLK), 2 * BLK, NB // 2)
    a_out = Phase(gate_u, a_w_out[0], (0, BLK), 2 * BLK, NB // 2)
    up0 = Phase(a_out, ffn_w_up[0], (0, FF), BLK, FP)
    down0 = Phase(up0, ffn_w_down[0], (0, BLK), 2 * BLK, NB // 2)
    q_in = Phase(down0, b_w_q[0], (0, BLK), 2 * BLK, NB // 2)
    k_in = Phase(q_in, w_k, (0, BLK), 2 * BLK, NB // 2)
    v_in = Phase(k_in, w_v, (0, BLK), 2 * BLK, NB // 2)
    b_out = Phase(v_in, b_w_o[0], (0, BLK), 2 * BLK, NB // 2)
    up1 = Phase(b_out, ffn_w_up[1], (0, FF), BLK, FP)
    down1 = Phase(up1, ffn_w_down[1], (0, BLK), 2 * BLK, NB // 2)
    phases = [gate_v, gate_u, a_out, up0, down0, q_in, k_in, v_in, b_out, up1, down1]
    UP, DOWN = (up0, up1), (down0, down1)
    NORMED = (a_out, down0, b_out, down1)
    POST_GAIN = (post_mix_g[0], post_ffn_g[0], post_mix_g[1], post_ffn_g[1])

    at = {"next": SBUF_START}

    def region(nbytes):
        start = at["next"]
        at["next"] += (nbytes + 31) // 32 * 32
        return start

    def place(name, shape, dtype, start):
        return nc.alloc_sbuf_tensor_at(name, [shape[0], *shape[1:]], dtype, offset=start)

    def sb(name, shape, dtype=F32):
        size = 4
        for n in shape[1:]:
            size *= n
        return place(name, shape, dtype, region(size))

    KB = 1024
    h = sb("h", [P, NH, D])
    raw = sb("raw", [P, RING, UK, BLK])
    w_hi = sb("w_hi", [P, RING, UK, BLK], F32R)
    w_lo = sb("w_lo", [P, RING, UK, BLK], F32R)

    x_at = region(32 * KB)
    x_parts = place("x_parts", [P, KT, 2, T], F32R, x_at)
    post_gain = place("post_gain", [P, D], F32, x_at)
    mixed = place("mixed", [P, NB, NH, BLK], F32, x_at + 16 * KB)
    att = place("att", [P, HEADS, ATT], F32, x_at)
    log_beta = place("log_beta", [P, 2, ATT], F32, x_at + 24 * KB)
    att_exp = place("att_exp", [P, 2, ATT], F32, x_at + 27 * KB)

    arena = region(FT * 2 * T * 4)
    u_t = place("u_t", [P, KT, T], F32, arena)
    v_nat = place("v_nat", [P, NH, G, P], F32, arena + 16 * KB)
    mix_parts = place("mix_parts", [P, KT, 2, T], F32R, arena + 32 * KB)
    ws_t = place("ws_t", [P, G, P], F32, arena + 64 * KB)
    v_gain = place("v_gain", [P, D], F32, arena + 72 * KB)
    bias_row = place("bias_row", [1, G, P], F32, arena + 72 * KB)
    v_square = place("v_square", [P, G, P], F32, arena + 80 * KB)
    ws_nat = place("ws_nat", [P, G, P], F32, arena + 32 * KB)
    gain_rows = place("gain_rows", [P, P], F32, arena + 40 * KB)
    conv_rows = place("conv_rows", [P, 2 * (TAPS + 1), P], F32, arena + 41 * KB)
    g_parts = place("g_parts", [P, FT, 2, T], F32R, arena)
    val = place("val", [P, NH, D], F32, arena)
    q_t = place("q_t", [P, HEADS, T], F32, arena + 16 * KB)
    k_t = place("k_t", [P, HEADS, T], F32, arena + 32 * KB)
    kv_parts = place("kv_parts", [P, KT, 2, T], F32R, arena + 48 * KB)
    o_parts = place("o_parts", [P, KT, 2, T], F32R, arena + 48 * KB)

    low = sb("low", [P, TB, T])
    conv_in = sb("conv_in", [P, TB, PAD + T])
    conv_at = region(TB * T * 4)
    conv = place("conv", [P, TB, T], F32, conv_at)
    v_sum = place("v_sum", [P, NH, G], F32, conv_at + KB)
    v_mean = place("v_mean", [P, NH, G], F32, conv_at + KB + 128)
    v_scale = place("v_scale", [P, NH, G], F32, conv_at + KB + 256)
    att_sp = place("att_sp", [P, 2, ATT], F32, conv_at)
    silu_at = region(TB * T * 4)
    silu = place("silu", [P, TB, T], F32, silu_at)
    att_log = place("att_log", [P, 2, ATT], F32, silu_at)
    diag = place("diag", [P, NH, P], F32, conv_at)
    junk = place("junk", [P, NH, BLK], F32, silu_at)

    ident = sb("ident", [P, P])
    later = sb("later", [P, P])
    ones = sb("ones", [P, P])
    row_scale = sb("row_scale", [P, T])
    mask = sb("mask", [P, ATT])
    NGAIN = 6 * KT
    gains = sb("gains", [P, NGAIN])
    conv_cols = sb("conv_cols", [P, 2, TAPS + 1, 2 * FT])
    half_neg = sb("half_neg", [P, KT * NH])
    block_sq = sb("block_sq", [P, NH, NB])
    post_sum = sb("post_sum", [P, NH])
    post_mean = sb("post_mean", [P, NH])
    post_scale = sb("post_scale", [P, NH])
    stream_sq = sb("stream_sq", [P, NH, NB])
    pre_sum = sb("pre_sum", [P, NH])
    pre_mean = sb("pre_mean", [P, NH])
    pre_scale = sb("pre_scale", [P, NH])
    assert at["next"] <= nc.sbuf_usable_end, at["next"] - nc.sbuf_usable_end

    GAIN_AT = {"mix0": 0, "mix1": KT, "ffn0": 2 * KT, "ffn1": 3 * KT, "kv": 4 * KT}
    PRE_GAIN = (("mix0",), ("ffn0",), ("mix1", "kv"), ("ffn1",))

    with ExitStack() as ctx:
        ps = ctx.enter_context(nc.psum_tensor("ps", [P, 8, BLK], F32))

        def sem(name):
            return ctx.enter_context(nc.semaphore(name))

        x_loaded = [sem(f"x_loaded{i}") for i in range(NH)]
        rows_loaded = sem("rows_loaded")
        spatial_loaded = sem("spatial_loaded")
        v_gain_loaded = sem("v_gain_loaded")
        bias_loaded = sem("bias_loaded")
        post_gain_loaded = sem("post_gain_loaded")
        constants = sem("constants")
        spatial_masked = sem("spatial_masked")
        rows_turned = sem("rows_turned")
        spatial_turned = sem("spatial_turned")
        columns_ready = sem("columns_ready")
        ws_ready = sem("ws_ready")
        raw_loaded = [sem(f"raw_loaded{i}") for i in range(RING)]
        unit_hi = sem("unit_hi")
        unit_split = sem("unit_split")
        unit_used = sem("unit_used")
        evacuated = sem("evacuated")
        low_copied = sem("low_copied")
        u_ready = sem("u_ready")
        v_step = sem("v_step")
        v_normed = sem("v_normed")
        group_mixed = sem("group_mixed")
        group_gated = sem("group_gated")
        group_hi = sem("group_hi")
        group_ready = sem("group_ready")
        half_done = sem("half_done")
        squared = sem("squared")
        post_meaned = sem("post_meaned")
        post_scaled = sem("post_scaled")
        h_new = sem("h_new")
        pre_squared = sem("pre_squared")
        pre_meaned = sem("pre_meaned")
        pre_scaled = sem("pre_scaled")
        diag_ready = sem("diag_ready")
        row_spread = sem("row_spread")
        row_ready = sem("row_ready")
        combined = sem("combined")
        x_turned = sem("x_turned")
        x_hi_ready = sem("x_hi_ready")
        x_ready = sem("x_ready")
        conv_step = sem("conv_step")
        silu_ready = sem("silu_ready")
        gated = sem("gated")
        g_hi_ready = sem("g_hi_ready")
        g_ready = sem("g_ready")
        scored = sem("scored")
        att_act = sem("att_act")
        att_dve = sem("att_dve")
        summed = sem("summed")
        weighted = sem("weighted")
        o_hi_ready = sem("o_hi_ready")
        o_ready = sem("o_ready")
        dve_order = sem("dve_order")
        stored = sem("stored")

        def token_bank(h_):
            return 2 * h_

        def column_bank(h_, flip=0):
            return 4 * ((h_ + flip) % 2)

        def turned(k):
            if k < 8:
                return ps[:, k, 0:T]
            return ps[:, 4 + (k - 8) // 2, (k % 2) * T:(k % 2 + 1) * T]

        def att_slot(n):
            part = {1: "scores", 2: "softplus", 0: "weights"}.get(n % 4)
            j = (n - RING - {"scores": 1, "softplus": 2, "weights": 4}.get(part, 0)) // 4
            return (part, j) if part and 0 <= j < STEPS else (None, None)

        block = ctx.enter_context(nc.Block())

        @block.sync
        def _(sp):
            def load_pair(ph, i, fresh=False):
                for hb in range(2):
                    for u in range(ph.units):
                        k = hb * ph.units + u
                        if not (fresh and k < RING):
                            sp.wait_ge(unit_split, i * (2 * ph.units) + (ph.first + k - RING + 1))
                        rows = ph.w[u * UK * P:(u + 1) * UK * P, bass.ds(ph.column(i, hb), BLK)]
                        sp.dma_start(raw[:, k % RING, :, :],
                                     rows.rearrange("(k p) n -> p k n", p=P)).then_inc(raw_loaded[k % RING], 16)

            for half in range(NH):
                sp.dma_start(h[:, half, :], x[0, half * P:(half + 1) * P, :]).then_inc(x_loaded[half], 16)
            for ph in phases:
                if ph is gate_v:
                    load_pair(ph, 0, fresh=True)
                with sp.Fori(1 if ph is gate_v else 0, ph.pairs) as i:
                    load_pair(ph, i)
            for c in range(NB):
                for half in range(NH):
                    sp.wait_ge(h_new, NH * NB * (len(NORMED) - 1) + NH * c + half + 1)
                    sp.dma_start(out[0, half * P:(half + 1) * P, c * BLK:(c + 1) * BLK],
                                 h[:, half, c * BLK:(c + 1) * BLK]).then_inc(stored, 16)
            sp.wait_ge(stored, 16 * NH * NB)

        @block.gpsimd
        def _(pool):
            pool.memset(half_neg[:, :], -0.5).then_inc(constants, 1)
            pool.memset(ident[:, :], 0.0).then_inc(constants, 1)
            pool.memset(ones[:, :], 1.0).then_inc(constants, 1)
            pool.memset(mask[:, :], 1.0).then_inc(constants, 1)
            pool.wait_ge(constants, 4)
            pool.affine_select(out=ident[:, :], in_=ident[:, :], compare_op=ALU.not_equal, fill=1.0,
                               base=0, pattern=[[-1, P]], channel_multiplier=1).then_inc(constants, 1)
            pool.affine_select(out=later[:, :], in_=ones[:, :], compare_op=ALU.is_gt, fill=0.0,
                               base=0, pattern=[[-1, P]], channel_multiplier=1).then_inc(constants, 1)
            for c in (0, T):
                pool.affine_select(out=mask[:, c:c + P], in_=mask[:, c:c + P], compare_op=ALU.is_gt, fill=0.0,
                                   base=0, pattern=[[1, P]], channel_multiplier=-1).then_inc(constants, 1)
            def rsqrt(to, of, n, ready, done, count):
                pool.wait_ge(ready, count)
                pool.tensor_tensor(to, of, half_neg[:, 0:n], ALU.pow).then_inc(done, 1)

            def pre_rsqrt(t):
                rsqrt(pre_scale[:, :], pre_mean[:, :], NH, pre_meaned, pre_scaled, t + 1)

            def load_post_gain(s):
                pool.dma_start(post_gain[:, :], POST_GAIN[s].unsqueeze(0).to_broadcast([P, D])
                               ).then_inc(post_gain_loaded, 16)

            pre_rsqrt(0)
            pool.wait_ge(spatial_loaded, 16)
            pool.affine_select(out=ws_nat[:, :, :], in_=ws_nat[:, :, :], compare_op=ALU.is_ge, fill=0.0,
                               base=0, pattern=[[0, G], [-1, P]], channel_multiplier=1).then_inc(spatial_masked, 1)
            pool.dma_start(v_gain[:, :], a_v_norm_g[0:1, :].to_broadcast([P, D])).then_inc(v_gain_loaded, 16)

            rsqrt(v_scale[:, :, :].rearrange("p a g -> p (a g)"), v_mean[:, :, :].rearrange("p a g -> p (a g)"),
                  NH * G, v_step, v_step, 5)
            for half in range(NH):
                pool.wait_ge(v_step, 7 + half)
                if half == 0:
                    pool.wait_ge(v_gain_loaded, 16)
                vh = v_nat[:, half, :, :].rearrange("p g d -> p (g d)")
                pool.tensor_tensor(vh, vh, v_gain[:, :], ALU.mult).then_inc(v_normed, 1)
            pool.wait_ge(v_normed, NH)
            pool.dma_start(bias_row[:, :, :], a_b_spatial).then_inc(bias_loaded, 16)
            for s, ph in enumerate(NORMED):
                if s == 2:
                    pool.wait_ge(weighted, STEPS)
                else:
                    pool.wait_ge(unit_used, ph.first)
                load_post_gain(s)
                for half in range(NH):
                    rsqrt(post_scale[:, half:half + 1], post_mean[:, half:half + 1], 1,
                          post_meaned, post_scaled, NH * s + half + 1)
                if s + 1 < len(NORMED):
                    pre_rsqrt(s + 1)

        @block.scalar
        def _(act):
            def units(base, a, b):
                for k in range(a, b):
                    slot = k % RING
                    if isinstance(base, int):
                        act.wait_ge(raw_loaded[slot], 16 * ((base + k) // RING + 1))
                    else:
                        act.wait_ge(raw_loaded[slot], base_loads[0] + 16 * (k // RING + 1))
                    if not isinstance(base, int) or base + k >= RING:
                        act.wait_ge(unit_used, base + (k - RING + 1))
                    act.copy(w_hi[:, slot, :, :], raw[:, slot, :, :]).then_inc(unit_hi, 1)

            base_loads = [None]

            def copy_low(ph, block_no, low_no, used, bank, scale=None):
                act.wait_ge(unit_used, used)
                act.wait_ge(evacuated, block_no)
                src = ps[:, bank:bank + TB, T:2 * T]
                ins = act.copy(low[:, :, :], src) if scale is None else act.mul(low[:, :, :], src, scale)
                ins.then_inc(low_copied, 1)

            def square(s, b):
                ph = NORMED[s]
                bank = token_bank(b % 2)
                if s + b:
                    act.wait_ge(squared, NH * (NB * s + b))
                for half in range(NH):
                    if half == 0:
                        act.wait_ge(half_done, NB * s + b + 1)
                    else:
                        act.wait_ge(unit_used, ph.unit(b + 1))
                    act.activation(junk[:, half, :], ps[:, bank + half, :], ACT.Square,
                                   accum_out=block_sq[:, half, b:b + 1]).then_inc(squared, 1)

            def square_stream(t, c):
                if t:
                    act.wait_ge(h_new, NH * (NB * (t - 1) + c + 1))
                    act.wait_ge(squared, NH * NB * t)
                if t + c:
                    act.wait_ge(pre_squared, NB * t + c)
                for half in range(NH):
                    if t == 0:
                        act.wait_ge(x_loaded[half], 16)
                    last = act.activation(junk[:, half, :], h[:, half, c * BLK:(c + 1) * BLK], ACT.Square,
                                          accum_out=stream_sq[:, half, c:c + 1])
                last.then_inc(pre_squared, 1)

            def x_high(t, tiles):
                for k in tiles:
                    act.wait_ge(x_turned, KT * t + (k + 1 if k < 8 else k // 2 * 2 + 2))
                    for name in PRE_GAIN[t]:
                        to = kv_parts if name == "kv" else x_parts
                        c = GAIN_AT[name] + k
                        ins = act.activation(to[:, k, HI, :], turned(k), ACT.Copy, scale=gains[:, c:c + 1])
                    ins.then_inc(x_hi_ready, 1)

            for row, g in ((0, pre_mix_g), (2 * KT, pre_ffn_g)):
                act.dma_start(gain_rows[row:row + 2 * KT, :], g.rearrange("l (k p) -> (l k) p", p=P)
                              ).then_inc(rows_loaded, 16)
            act.dma_start(gain_rows[4 * KT:5 * KT, :], kv_norm_g.rearrange("(k p) -> k p", p=P)).then_inc(rows_loaded, 16)
            act.dma_start(gain_rows[5 * KT:6 * KT, :], a_v_norm_g[0].rearrange("(k p) -> k p", p=P)
                          ).then_inc(rows_loaded, 16)
            for layer in range(2):
                r = layer * (TAPS + 1)
                act.dma_start(conv_rows[0:2 * FT, r:r + TAPS, :], ffn_conv_w[layer].rearrange("t (f p) -> f t p", p=P)
                              ).then_inc(rows_loaded, 16)
                act.dma_start(conv_rows[0:2 * FT, r + TAPS, :], ffn_conv_b[layer].rearrange("(f p) -> f p", p=P)
                              ).then_inc(rows_loaded, 16)
            act.dma_start(ws_nat[:, :, :], a_w_spatial[0].rearrange("g t s -> t g s")).then_inc(spatial_loaded, 16)
            def turn_and_split(t, ph):
                for c in range(NB - 1):
                    x_high(t, range(c * TB, (c + 1) * TB))
                    square_stream(t, c)
                square_stream(t, NB - 1)
                units(ph.first, RING, RING + 2)
                x_high(t, range((NB - 1) * TB, KT))
                units(ph.first, RING + 2, ph.units)

            units(0, 0, RING)
            turn_and_split(0, gate_v)

            def gelu_v(b):
                act.wait_ge(unit_used, gate_v.unit(b + 1))
                act.wait_ge(pre_scaled, 1)
                bank = token_bank(b % 2)
                for half in range(NH):
                    last = act.activation(v_nat[:, half, b * TB:(b + 1) * TB, :].rearrange("p g d -> p (g d)"),
                                          ps[:, bank + half, :], ACT.Gelu_apprx_tanh,
                                          scale=pre_scale[:, half:half + 1])
                last.then_inc(evacuated, 1)

            def gelu_u(b):
                act.wait_ge(combined, b + 1)
                tiles = u_t[:, b * TB:(b + 1) * TB, :]
                act.activation(tiles, tiles, ACT.Gelu_apprx_tanh).then_inc(u_ready, 1)

            U = gate_v.units
            for b in range(1, NB):
                units(gate_v.unit(b), 0, RING)
                gelu_v(b - 1)
                if b == 2:
                    act.wait_ge(spatial_turned, 1)
                    act.copy(ws_t[:, :, :].rearrange("p (b g) s -> p b (g s)", b=4), ps[:, 4:8, :]
                             ).then_inc(ws_ready, 1)
                units(gate_v.unit(b), RING, U)
            for b in range(NB):
                units(gate_u.unit(b), 0, RING)
                if b == 0:
                    gelu_v(LAST)
                    units(gate_u.unit(b), RING, U)
                else:
                    copy_low(gate_u, gate_u.block0 + b - 1, b, gate_u.unit(b), column_bank(b - 1, 1))
                    units(gate_u.unit(b), RING, RING + 2)
                    gelu_u(b - 1)
                    units(gate_u.unit(b), RING + 2, U)

            def group_high(g2):
                act.wait_ge(group_gated, g2 + 1)
                act.copy(mix_parts[:, 2 * g2:2 * g2 + 2, HI, :], v_square[:, :, :].rearrange(
                    "p g d -> p (g d)")[:, (g2 % 4) * 2 * T:(g2 % 4 + 1) * 2 * T].rearrange("p (g t) -> p g t", g=2)
                         ).then_inc(group_hi, 1)

            units(a_out.first, 0, RING)
            copy_low(gate_u, gate_u.block_end - 1, NB, gate_u.end, column_bank(LAST % 2, 1))
            for g2 in range(3):
                group_high(g2)
            gelu_u(LAST)
            for g2 in range(3, 4):
                group_high(g2)
            for g2 in range(4, 8):
                units(a_out.first, g2, g2 + 1)
                group_high(g2)
            for b in range(1, NB):
                units(a_out.unit(b), 0, RING)
                square(0, b - 1)
                units(a_out.unit(b), RING, U)

            def after_normed(s, nxt):
                units(nxt.first, 0, RING)
                square(s, LAST)
                turn_and_split(s + 1, nxt)

            def ffn_gate_silu(ff_block, j):
                act.wait_ge(conv_step, 3 * ff_block + 3)
                if not isinstance(j, int) or j:
                    act.wait_ge(gated, j)
                act.activation(silu[:, :, :], conv[:, :, :], ACT.Silu).then_inc(silu_ready, 1)

            def ffn_high(layer, i):
                act.wait_ge(gated, i + layer * FP + 1)
                act.copy(g_parts[:, bass.ds(i * TB, TB), HI, :], conv[:, :, :]).then_inc(g_hi_ready, 1)

            def ffn_up(layer, s):
                ph = UP[layer]
                low0 = 4 + 8 * layer + 2 * FP * layer

                def gate_part(i):
                    base = i * (2 * U) + ph.first
                    units(base, U, U + RING)
                    copy_low(ph, i * 2 + ph.block0, None, base + U, column_bank(0))
                    units(base, U + RING, 2 * U)
                    ffn_gate_silu(i * 2 + 2 * FP * layer, i + FP * layer)

                def value_part(i, base, last):
                    copy_low(ph, i * 2 + (ph.block0 + 1), None, i * (2 * U) + (ph.first + 2 * U), column_bank(1))
                    units(base, RING, last - 1)
                    ffn_high(layer, i)
                    units(base, last - 1, last)

                after_normed(s, ph)
                gate_part(0)
                with act.Fori(1, ph.pairs) as i:
                    base = i * (2 * U) + ph.first
                    base_loads[0] = i * (16 * 2 * U // RING) + 16 * ph.first // RING
                    units(base, 0, RING)
                    copy_low(ph, i * 2 + (ph.block0 - 1), None, base, column_bank(1))
                    units(base, RING, U - 1)
                    ffn_high(layer, i - 1)
                    units(base, U - 1, U)
                    gate_part(i)

            def ffn_down(layer, s):
                ph, up = DOWN[layer], UP[layer]
                units(ph.first, 0, RING)
                copy_low(up, up.block_end - 1, None, up.end, column_bank(1))
                units(ph.first, RING, U - 1)
                ffn_high(layer, FP - 1)
                units(ph.first, U - 1, ph.units)
                for b in range(1, NB):
                    units_of(ph, b, 0, RING)
                    square(s, b - 1)
                    units_of(ph, b, RING, ph.units)

            def units_of(ph, b, a, e):
                units(ph.first, b * ph.units + a, b * ph.units + e)

            ffn_up(0, 0)
            ffn_down(0, 1)

            after_normed(1, q_in)
            for ph in (q_in, k_in):
                for b in range(NB):
                    if ph is q_in and b == 0:
                        continue
                    units(ph.unit(b), 0, RING)
                    done, bank = ph.block0 + b - 1, column_bank((b + 1) % 2)
                    scaled = (ph is q_in) or b == 0
                    copy_low(ph, done, None, ph.unit(b), bank, SCALE if scaled else None)
                    units(ph.unit(b), RING, U)

            def copy_value(b):
                act.wait_ge(unit_used, v_in.unit(b + 1))
                bank = token_bank(b % 2)
                for half in range(NH):
                    last = act.activation(val[:, half, b * BLK:(b + 1) * BLK], ps[:, bank + half, :], ACT.Copy,
                                          scale=pre_scale[:, half:half + 1])
                last.then_inc(evacuated, 1)

            def att_softplus_1(j):
                act.wait_ge(scored, j + 1)
                if j:
                    act.wait_ge(att_dve, 5 * (j - 1) + 3)
                act.activation(att_log[:, :, :], ps[:, 4:6, 0:ATT], ACT.Abs).then_inc(att_act, 1)
                act.wait_ge(att_act, 4 * j + 1)
                act.activation(att_log[:, :, :], att_log[:, :, :], ACT.Exp, scale=-1.0).then_inc(att_act, 1)

            def att_softplus_2(j):
                act.wait_ge(att_act, 4 * j + 2)
                act.activation(att_log[:, :, :], att_log[:, :, :], ACT.Ln, bias=1.0).then_inc(att_act, 1)

            def att_weight(j):
                act.wait_ge(att_dve, 5 * j + 4)
                act.activation(att_exp[:, :, :], att_exp[:, :, :], ACT.Exp).then_inc(att_act, 1)

            for n in range(v_in.units * NB + RING):
                ph = v_in if n < v_in.units * NB else b_out
                units(v_in.first, n, n + 1)
                if n == RING - 1:
                    copy_low(k_in, k_in.block_end - 1, None, k_in.end, column_bank(1))
                if n >= U + RING - 1 and (n - RING + 1) % U == 0:
                    copy_value((n - RING + 1) // U - 1)
                part, j = att_slot(n)
                if part == "scores":
                    att_softplus_1(j)
                elif part == "softplus":
                    att_softplus_2(j)
                elif part == "weights":
                    att_weight(j)
            att_weight(STEPS - 1)

            def out_high(j):
                act.wait_ge(weighted, j + 1)
                act.copy(o_parts[:, 2 * j:2 * j + 2, HI, :], ps[:, j, :].rearrange("p (a t) -> p a t", a=2)
                         ).then_inc(o_hi_ready, 1)

            for j in range(4):
                out_high(j)
            for j in range(4, 8):
                units(b_out.first, j, j + 1)
                out_high(j)
            for b in range(1, NB):
                units(b_out.unit(b), 0, RING)
                square(2, b - 1)
                units(b_out.unit(b), RING, U)

            ffn_up(1, 2)
            ffn_down(1, 3)
            square(3, LAST)

        @block.vector
        def _(dve):
            def units(base, a, b):
                for k in range(a, b):
                    slot = k % RING
                    dve.wait_ge(unit_hi, base + (k + 1))
                    dve.tensor_tensor(w_lo[:, slot, :, :], raw[:, slot, :, :], w_hi[:, slot, :, :].bitcast(F32),
                                      ALU.subtract).then_inc(unit_split, 1)

            ordered = [0]

            def link(ins):
                ordered[0] += 1
                ins.then_inc(dve_order, 1)
                dve.wait_ge(dve_order, ordered[0])

            def add_low(to, low_no, bank, scale=None):
                dve.wait_ge(low_copied, low_no)
                src = ps[:, bank:bank + TB, 0:T]
                if scale is None:
                    dve.tensor_tensor(to, src, low[:, :, :], ALU.add).then_inc(evacuated, 1)
                else:
                    dve.scalar_tensor_tensor(out=to, in0=src, scalar=scale, in1=low[:, :, :],
                                             op0=ALU.mult, op1=ALU.add).then_inc(evacuated, 1)

            def scale_tokens(to, block_no, low_no):
                dve.wait_ge(evacuated, block_no + 1)
                dve.tensor_tensor(to, to, row_scale[:, :].unsqueeze(1).to_broadcast([P, TB, T]), ALU.mult
                                  ).then_inc(combined, 1)

            def gain_block(s, b):
                dve.wait_ge(post_gain_loaded, 16 * (s + 1))
                bank = token_bank(b % 2)
                for half in range(NH):
                    dve.wait_ge(squared, NH * (NB * s + b) + half + 1)
                    last = dve.tensor_tensor(mixed[:, b, half, :], ps[:, bank + half, :],
                                             post_gain[:, b * BLK:(b + 1) * BLK], ALU.mult)
                last.then_inc(evacuated, 1)

            def post_norm(s):
                for half in range(NH):
                    dve.wait_ge(squared, NH * (NB * s + LAST) + half + 1)
                    link(dve.tensor_reduce(post_sum[:, half:half + 1], block_sq[:, half, :], AX.X, ALU.add))
                    dve.tensor_scalar(post_mean[:, half:half + 1], post_sum[:, half:half + 1], 1.0 / D, EPS,
                                      ALU.mult, ALU.add).then_inc(post_meaned, 1)
                gain_block(s, LAST)

            def update_stream(s, c):
                for half in range(NH):
                    if c == 0:
                        dve.wait_ge(post_scaled, NH * s + half + 1)
                        dve.wait_ge(evacuated, NORMED[s].block_end)
                    hc = h[:, half, c * BLK:(c + 1) * BLK]
                    dve.scalar_tensor_tensor(out=hc, in0=mixed[:, c, half, :],
                                             scalar=post_scale[:, half:half + 1], in1=hc,
                                             op0=ALU.mult, op1=ALU.add).then_inc(h_new, 1)

            def pre_means(t):
                dve.wait_ge(pre_squared, NB * (t + 1))
                link(dve.tensor_reduce(pre_sum[:, :], stream_sq[:, :, :], AX.X, ALU.add))
                dve.tensor_scalar(pre_mean[:, :], pre_sum[:, :], 1.0 / D, EPS, ALU.mult, ALU.add
                                  ).then_inc(pre_meaned, 1)

            def pre_diagonals(t):
                dve.wait_ge(pre_scaled, t + 1)
                for half in range(NH):
                    last = dve.tensor_scalar(diag[:, half, :], ident[:, :], pre_scale[:, half:half + 1], None, ALU.mult)
                last.then_inc(diag_ready, 1)

            def turn_and_split(t, ph):
                for c in range(NB - 1):
                    if t:
                        update_stream(t - 1, c)
                    x_low(t, range(c * TB, (c + 1) * TB))
                if t:
                    update_stream(t - 1, NB - 1)
                units(ph.first, RING, RING + 2)
                pre_means(t)
                x_low(t, range((NB - 1) * TB, KT))
                pre_diagonals(t)
                units(ph.first, RING + 2, ph.units)

            def copy_row_scale(t):
                dve.wait_ge(row_spread, t + 1)
                dve.tensor_copy(row_scale[:, :], ps[:, 4, 0:T]).then_inc(row_ready, 1)

            def x_low(t, tiles):
                for k in tiles:
                    dve.wait_ge(x_hi_ready, KT * t + (k + 1 if k < 8 else k // 2 * 2 + 2))
                    for name in PRE_GAIN[t]:
                        to = kv_parts if name == "kv" else x_parts
                        c = GAIN_AT[name] + k
                        ins = dve.scalar_tensor_tensor(out=to[:, k, LO, :], in0=turned(k), scalar=gains[:, c:c + 1],
                                                       in1=to[:, k, HI, :].bitcast(F32),
                                                       op0=ALU.mult, op1=ALU.subtract)
                    ins.then_inc(x_ready, 1)

            link(dve.memset(conv_in[:, :, 0:PAD], 0.0))
            dve.wait_ge(rows_turned, 1)
            dve.tensor_copy(gains[:, :], ps[:, 6, 0:NGAIN]).then_inc(columns_ready, 1)
            dve.tensor_copy(conv_cols[:, :, :, :].rearrange("p l t f -> p l (t f)"),
                            ps[:, 4:6, 0:(TAPS + 1) * 2 * FT]).then_inc(columns_ready, 1)
            units(0, 0, RING)
            dve.wait_ge(columns_ready, 2)
            turn_and_split(0, gate_v)
            U = gate_v.units
            units(gate_v.unit(1), 0, 2)
            copy_row_scale(0)
            units(gate_v.unit(1), 2, U)
            for b in range(2, NB):
                units(gate_v.unit(b), 0, U)

            def square_v(half):
                if half == 0:
                    dve.wait_ge(evacuated, gate_v.block_end)
                dve.tensor_tensor(v_square[:, :, :], v_nat[:, half, :, :], v_nat[:, half, :, :], ALU.mult
                                  ).then_inc(v_step, 1)

            def sum_v(half):
                dve.wait_ge(v_step, 2 * half + 1)
                dve.tensor_reduce(v_sum[:, half, :], v_square[:, :, :], AX.X, ALU.add).then_inc(v_step, 1)

            def mean_v():
                dve.wait_ge(v_step, 4)
                dve.tensor_scalar(v_mean[:, :, :], v_sum[:, :, :], 1.0 / P, EPS, ALU.mult, ALU.add
                                  ).then_inc(v_step, 1)

            def norm_v(half):
                dve.wait_ge(v_step, 6)
                dve.tensor_tensor(v_nat[:, half, :, :], v_nat[:, half, :, :],
                                  v_scale[:, half, :].unsqueeze(2).to_broadcast([P, G, P]), ALU.mult
                                  ).then_inc(v_step, 1)

            def add_u(b):
                to = u_t[:, b * TB:(b + 1) * TB, :]
                add_low(to, b + 1, column_bank(b % 2, 1))
                scale_tokens(to, gate_u.block0 + b, b + 1)

            units(gate_u.unit(0), 0, RING)
            square_v(0)
            units(gate_u.unit(0), RING, RING + 1)
            sum_v(0)
            units(gate_u.unit(0), RING + 1, RING + 2)
            dve.wait_ge(v_step, 2)
            square_v(1)
            units(gate_u.unit(0), RING + 2, RING + 3)
            sum_v(1)
            units(gate_u.unit(0), RING + 3, U)
            mean_v()
            units(gate_u.unit(1), 0, RING)
            add_u(0)
            units(gate_u.unit(1), RING, RING + 1)
            norm_v(0)
            units(gate_u.unit(1), RING + 1, RING + 3)
            norm_v(1)
            units(gate_u.unit(1), RING + 3, U)
            for b in range(2, NB):
                units(gate_u.unit(b), 0, RING)
                add_u(b - 1)
                units(gate_u.unit(b), RING, U)

            def gate_place(g2):
                return v_square[:, :, :].rearrange("p g d -> p (g d)")[:, (g2 % 4) * 2 * T:(g2 % 4 + 1) * 2 * T]

            def gate_group(g2):
                dve.wait_ge(group_mixed, g2 + 1)
                dve.wait_ge(u_ready, g2 // 2 + 1)
                dve.tensor_tensor(gate_place(g2), ps[:, g2, :],
                                  u_t[:, 2 * g2:2 * g2 + 2, :].rearrange("p g t -> p (g t)"), ALU.mult
                                  ).then_inc(group_gated, 1)

            def group_low(g2):
                dve.wait_ge(group_hi, g2 + 1)
                dve.tensor_tensor(mix_parts[:, 2 * g2:2 * g2 + 2, LO, :],
                                  gate_place(g2).rearrange("p (g t) -> p g t", g=2),
                                  mix_parts[:, 2 * g2:2 * g2 + 2, HI, :].bitcast(F32), ALU.subtract
                                  ).then_inc(group_ready, 1)

            units(a_out.first, 0, RING)
            add_u(LAST)
            for g2 in range(4):
                gate_group(g2)
                if g2:
                    group_low(g2 - 1)
            for g2 in range(4, 8):
                group_low(g2 - 1)
                gate_group(g2)
                units(a_out.first, g2, g2 + 1)
            group_low(7)
            for b in range(1, NB):
                units(a_out.unit(b), 0, RING)
                gain_block(0, b - 1)
                units(a_out.unit(b), RING, U)

            def after_normed(s, nxt):
                units(nxt.first, 0, RING)
                post_norm(s)
                turn_and_split(s + 1, nxt)

            def ffn_taps(layer, i, part, tap, ff_block):
                for m in range(TB):
                    tile = i * TB + (part * FT + m)
                    w = conv_cols[:, layer, tap, bass.ds(tile, 1)]
                    src = conv_in[:, m, tap:tap + T]
                    if tap == PAD:
                        ins = dve.tensor_scalar(conv[:, m, :], src, w, conv_cols[:, layer, TAPS, bass.ds(tile, 1)],
                                                ALU.mult, ALU.add)
                    else:
                        ins = dve.scalar_tensor_tensor(out=conv[:, m, :], in0=src, scalar=w, in1=conv[:, m, :],
                                                       op0=ALU.mult, op1=ALU.add)
                ins.then_inc(conv_step, 1)

            def ffn_block(layer, i, part, base, a, e):
                ff = i * 2 + (2 * FP * layer + part)
                low_no = i * 2 + (2 * FP * layer + part + NB + 2 * NB * layer + 1)
                add_low(conv_in[:, :, PAD:PAD + T], low_no, column_bank(part))
                scale_tokens(conv_in[:, :, PAD:PAD + T], i * 2 + (UP[layer].block0 + part), low_no)
                units(base, a + RING, a + RING + 1)
                dve.wait_ge(combined, low_no)
                if part:
                    dve.wait_ge(silu_ready, i + (layer * FP + 1))
                ffn_taps(layer, i, part, 2, ff)
                units(base, a + RING + 1, a + RING + 2)
                dve.wait_ge(conv_step, ff * 3 + 1)
                ffn_taps(layer, i, part, 1, ff)
                units(base, a + RING + 2, a + RING + 3)
                dve.wait_ge(conv_step, ff * 3 + 2)
                ffn_taps(layer, i, part, 0, ff)
                if part:
                    dve.wait_ge(conv_step, ff * 3 + 3)
                    dve.tensor_tensor(conv[:, :, :], conv[:, :, :], silu[:, :, :], ALU.mult).then_inc(gated, 1)
                units(base, a + RING + 3, e)
                if part:
                    dve.wait_ge(g_hi_ready, i + (layer * FP + 1))
                    dve.tensor_tensor(g_parts[:, bass.ds(i * TB, TB), LO, :], conv[:, :, :],
                                      g_parts[:, bass.ds(i * TB, TB), HI, :].bitcast(F32), ALU.subtract
                                      ).then_inc(g_ready, 1)

            def ffn_up(layer, s):
                ph = UP[layer]
                after_normed(s, ph)
                units(ph.first, U, U + 2)
                copy_row_scale(s + 1)
                units(ph.first, U + 2, U + RING)
                ffn_block(layer, 0, 0, ph.first, U, 2 * U)
                with dve.Fori(1, ph.pairs) as i:
                    base = i * (2 * U) + ph.first
                    units(base, 0, RING)
                    ffn_block(layer, i - 1, 1, base, 0, U)
                    units(base, U, U + RING)
                    ffn_block(layer, i, 0, base, U, 2 * U)

            def ffn_down(layer, s):
                ph = DOWN[layer]
                units(ph.first, 0, RING)
                ffn_block(layer, FP - 1, 1, ph.first, 0, U)
                units(ph.first, U, ph.units)
                for b in range(1, NB):
                    k = b * ph.units
                    units(ph.first, k, k + RING)
                    gain_block(s, b - 1)
                    units(ph.first, k + RING, k + ph.units)

            ffn_up(0, 0)
            ffn_down(0, 1)

            after_normed(1, q_in)
            low_no = NB + 2 * FP
            for ph in (q_in, k_in):
                for b in range(NB):
                    if ph is q_in and b == 0:
                        continue
                    units(ph.unit(b), 0, 2)
                    if low_no == NB + 2 * FP:
                        copy_row_scale(2)
                    units(ph.unit(b), 2, RING)
                    low_no += 1
                    to, c = (q_t, (b - 1) % NB) if (ph is q_in or b == 0) else (k_t, b - 1)
                    to_block = to[:, c * TB:(c + 1) * TB, :]
                    add_low(to_block, low_no, column_bank((b + 1) % 2), SCALE if to is q_t else None)
                    scale_tokens(to_block, ph.block0 + b - 1, low_no)
                    units(ph.unit(b), RING, U)

            def att_softplus(j):
                dve.wait_ge(att_act, 4 * j + 3)
                if j:
                    dve.wait_ge(summed, j)
                dve.scalar_tensor_tensor(out=att_sp[:, :, :], in0=ps[:, 4:6, 0:ATT], scalar=0.0, in1=att_log[:, :, :],
                                         op0=ALU.max, op1=ALU.add).then_inc(att_dve, 1)
                dve.wait_ge(att_dve, 5 * j + 1)
                dve.tensor_tensor(att_sp[:, :, :], att_sp[:, :, :],
                                  mask[:, :].unsqueeze(1).to_broadcast([P, 2, ATT]), ALU.mult).then_inc(att_dve, 1)
                dve.scalar_tensor_tensor(out=log_beta[:, :, :], in0=ps[:, 4:6, 0:ATT], scalar=0.0,
                                         in1=att_log[:, :, :], op0=ALU.min, op1=ALU.subtract).then_inc(att_dve, 1)

            def att_exponent(j):
                dve.wait_ge(summed, j + 1)
                dve.wait_ge(att_dve, 5 * j + 3)
                dve.tensor_tensor(att_exp[:, :, :], log_beta[:, :, :], ps[:, 6:8, 0:ATT], ALU.subtract
                                  ).then_inc(att_dve, 1)
                dve.wait_ge(att_act, 4 * j + 4)
                dve.tensor_tensor(att[:, 2 * j:2 * j + 2, :], att_exp[:, :, :],
                                  mask[:, :].unsqueeze(1).to_broadcast([P, 2, ATT]), ALU.mult).then_inc(att_dve, 1)

            for n in range(v_in.units * NB + RING):
                units(v_in.first, n, n + 1)
                if n == RING - 1:
                    add_low(k_t[:, LAST * TB:(LAST + 1) * TB, :], low_no + 1, column_bank(1))
                    scale_tokens(k_t[:, LAST * TB:(LAST + 1) * TB, :], k_in.block_end - 1, low_no + 1)
                part, j = att_slot(n)
                if part == "softplus":
                    att_softplus(j)
                elif part == "weights":
                    att_exponent(j)
            att_exponent(STEPS - 1)

            def out_low(j):
                dve.wait_ge(o_hi_ready, j + 1)
                dve.tensor_tensor(o_parts[:, 2 * j:2 * j + 2, LO, :], ps[:, j, :].rearrange("p (a t) -> p a t", a=2),
                                  o_parts[:, 2 * j:2 * j + 2, HI, :].bitcast(F32), ALU.subtract).then_inc(o_ready, 1)

            for j in range(4):
                out_low(j)
            for j in range(4, 8):
                units(b_out.first, j, j + 1)
                out_low(j)
            for b in range(1, NB):
                units(b_out.unit(b), 0, RING)
                gain_block(2, b - 1)
                units(b_out.unit(b), RING, U)

            ffn_up(1, 2)
            ffn_down(1, 3)
            post_norm(3)
            for c in range(NB):
                update_stream(3, c)

        @block.tensor
        def _(pe):
            def columns_out(ph, i, src, ready, first_ready, flip=0, t=None):
                for hb in range(2):
                    bank = column_bank(hb, flip)
                    for u in range(ph.units):
                        k = hb * ph.units + u
                        slot = k % RING
                        pe.wait_ge(unit_split, i * (2 * ph.units) + (ph.first + k + 1))
                        pe.wait_ge(ready, first_ready + UK * u + UK)
                        if u == 0:
                            pe.wait_ge(evacuated, i * 2 + (ph.block0 + hb - 1))
                            if t is not None and hb:
                                pe.wait_ge(row_ready, t + 1)
                        for m in range(TB):
                            for kk in range(UK):
                                kt = UK * u + kk
                                first, last = kt == 0, kt == KT - 1
                                pe.matmul(ps[:, bank + m, :], w_hi[:, slot, kk, m * P:(m + 1) * P],
                                          src[:, kt, :, :].rearrange("p a t -> p (a t)"), start=first, stop=False,
                                          skip_group_check=True)
                                mm = pe.matmul(ps[:, bank + m, 0:T], w_lo[:, slot, kk, m * P:(m + 1) * P],
                                               src[:, kt, HI, :], start=False, stop=last, skip_group_check=True)
                        mm.then_inc(unit_used, 1)
                        if t is not None and hb == 0:
                            turn_rest(t, u)

            def tokens_out_unit(ph, i, hb, u, src, bank):
                k = hb * ph.units + u
                slot = k % RING
                for half in range(NH):
                    t0 = half * P
                    for kk in range(UK):
                        kt = UK * u + kk
                        first, last = kt == 0, kt == UK * ph.units - 1
                        to = ps[:, bank + half, :]
                        pe.matmul(to, src[:, kt, HI, t0:t0 + P], w_hi[:, slot, kk, :], start=first, stop=False)
                        pe.matmul(to, src[:, kt, HI, t0:t0 + P], w_lo[:, slot, kk, :], start=False, stop=False)
                        mm = pe.matmul(to, src[:, kt, LO, t0:t0 + P], w_hi[:, slot, kk, :], start=False, stop=last)
                    if half == 0 and last and ph in NORMED:
                        mm.then_inc(half_done, 1)
                mm.then_inc(unit_used, 1)

            def tokens_out(ph, i, src, ready, count, t=None):
                for hb in range(2):
                    for u in range(ph.units):
                        pe.wait_ge(unit_split, i * (2 * ph.units) + (ph.first + hb * ph.units + u + 1))
                        pe.wait_ge(ready, count(u))
                        if u == 0 and t != 0:
                            pe.wait_ge(evacuated, i * 2 + (ph.block0 + hb - 1))
                        tokens_out_unit(ph, i, hb, u, src, token_bank(hb))
                        if t is not None and hb == 0:
                            turn_rest(t, u)

            def turn(t, tiles):
                for k in tiles:
                    if k % TB == 0:
                        if t:
                            pe.wait_ge(h_new, NH * (NB * (t - 1) + k // TB + 1))
                        else:
                            pe.wait_ge(x_loaded[0], 16)
                            pe.wait_ge(x_loaded[1], 16)
                    if k >= 8:
                        pe.wait_ge(x_ready, KT * t + 4 + (k - 8) // 2 + 1)
                    for half in range(NH):
                        tr = pe.transpose(turned(k)[:, half * P:(half + 1) * P], h[:, half, k * P:(k + 1) * P],
                                          ident[:, :])
                    tr.then_inc(x_turned, 1)

            def turn_rest(t, u):
                if u == 1:
                    turn(t, range(8, 12))
                if u == 3:
                    turn(t, range(12, KT))
                if u == 5:
                    pe.wait_ge(diag_ready, t + 1)
                    for half in range(NH):
                        mm = pe.matmul(ps[:, 4, half * P:(half + 1) * P], ones[:, :], diag[:, half, :],
                                       start=True, stop=True)
                    mm.then_inc(row_spread, 1)

            def turn_first(t):
                turn(t, range(0, 8))
                pe.wait_ge(x_ready, KT * t + 4)

            pe.wait_ge(constants, 8)
            pe.wait_ge(rows_loaded, 16 * 8)
            for r in range(2 * (TAPS + 1)):
                c = (r % (TAPS + 1)) * 2 * FT
                pe.transpose(ps[:, 4 + r // (TAPS + 1), c:c + 2 * FT], conv_rows[0:2 * FT, r, :],
                             ident[0:2 * FT, 0:2 * FT])
            pe.transpose(ps[:, 6, 0:NGAIN], gain_rows[0:NGAIN, :], ident[0:NGAIN, 0:NGAIN]).then_inc(rows_turned, 1)
            pe.wait_ge(columns_ready, 2)
            turn_first(0)
            tokens_out(gate_v, 0, x_parts, x_ready, lambda u: UK * u + UK, t=0)
            pe.wait_ge(spatial_masked, 1)
            pe.wait_ge(row_ready, 1)
            for g in range(G):
                tr = pe.transpose(ps[:, 4 + g // 4, (g % 4) * P:(g % 4 + 1) * P], ws_nat[:, g, :], ident[:, :])
            tr.then_inc(spatial_turned, 1)
            with pe.Fori(1, gate_v.pairs) as i:
                tokens_out(gate_v, i, x_parts, x_ready, lambda u: UK * u + UK)
            pe.wait_ge(ws_ready, 1)
            with pe.Fori(0, gate_u.pairs) as i:
                columns_out(gate_u, i, x_parts, x_ready, 0, flip=1)

            pe.wait_ge(v_normed, NH)
            pe.wait_ge(bias_loaded, 16)
            pe.wait_ge(evacuated, gate_u.block_end)
            for g2 in range(G // 2):
                for j in range(4):
                    pe.matmul(ps[:, g2, j * P:(j + 1) * P], ones[0:1, :], bias_row[0:1, 2 * g2 + j // 2, :],
                              start=(j == 0), stop=False, skip_group_check=True)
                for j in range(4):
                    g, chunk = 2 * g2 + j // 2, j % 2
                    mm = pe.matmul(ps[:, g2, j * P:(j + 1) * P], v_nat[:, chunk, g, :], ws_t[:, g, :],
                                   start=False, stop=(j == 3), skip_group_check=True)
                mm.then_inc(group_mixed, 1)
            pe.wait_ge(group_gated, 4)
            with pe.Fori(0, a_out.pairs) as i:
                tokens_out(a_out, i, mix_parts, group_ready, lambda u: u + 1)

            for layer in range(2):
                t = 1 + 2 * layer
                turn_first(t)
                columns_out(UP[layer], 0, x_parts, x_ready, KT * t, t=t)
                with pe.Fori(1, FP) as i:
                    columns_out(UP[layer], i, x_parts, x_ready, KT * t)
                with pe.Fori(0, DOWN[layer].pairs) as i:
                    tokens_out(DOWN[layer], i, g_parts, g_ready, lambda u: layer * FP + (UK * u + 1) // TB + 1)
                if layer == 1:
                    break

                turn_first(2)
                columns_out(q_in, 0, x_parts, x_ready, KT * 2, t=2)
                with pe.Fori(1, q_in.pairs) as i:
                    columns_out(q_in, i, x_parts, x_ready, KT * 2)
                with pe.Fori(0, k_in.pairs) as i:
                    columns_out(k_in, i, kv_parts, x_ready, KT * 2)

                def score(j):
                    pe.wait_ge(combined, NB + 2 * FP + 2 * NB)
                    if j:
                        pe.wait_ge(att_dve, 5 * (j - 1) + 3)
                    for a in range(2):
                        hd = 2 * j + a
                        pe.matmul(ps[:, 4 + a, 0:T], k_t[:, hd, 0:P], q_t[:, hd, :], start=True, stop=True)
                        mm = pe.matmul(ps[:, 4 + a, T:ATT], k_t[:, hd, P:T], q_t[:, hd, P:T], start=True, stop=True)
                    mm.then_inc(scored, 1)

                def sum_later(j):
                    pe.wait_ge(att_dve, 5 * j + 2)
                    if j:
                        pe.wait_ge(att_dve, 5 * (j - 1) + 4)
                    for a in range(2):
                        pe.matmul(ps[:, 6 + a, 0:ATT], later[:, :], att_sp[:, a, :], start=True, stop=False,
                                  skip_group_check=True)
                        mm = pe.matmul(ps[:, 6 + a, P:T], ones[:, :], att_sp[:, a, T:ATT], start=False, stop=True,
                                       skip_group_check=True)
                    mm.then_inc(summed, 1)

                for n in range(v_in.units * NB):
                    hb, u = n // v_in.units % 2, n % v_in.units
                    pe.wait_ge(unit_split, v_in.first + n + 1)
                    if u == 0:
                        pe.wait_ge(evacuated, v_in.block0 + n // v_in.units - 1)
                    tokens_out_unit(v_in, 0, hb, u, kv_parts, token_bank(hb))
                    if n % 4 == 0 and n:
                        sum_later(n // 4 - 1)
                    if n % 4 == 0:
                        score(n // 4)
                sum_later(STEPS - 1)
                pe.wait_ge(evacuated, v_in.block_end)
                pe.wait_ge(att_dve, 5 * STEPS)
                for j in range(STEPS):
                    for a in range(2):
                        hd = 2 * j + a
                        pe.matmul(ps[:, j, a * T:(a + 1) * T], val[:, 0, hd * P:(hd + 1) * P], att[:, hd, 0:T],
                                  start=True, stop=False, skip_group_check=True)
                        mm = pe.matmul(ps[:, j, a * T + P:(a + 1) * T], val[:, 1, hd * P:(hd + 1) * P],
                                       att[:, hd, T:ATT], start=False, stop=True, skip_group_check=True)
                    mm.then_inc(weighted, 1)
                pe.wait_ge(o_ready, 4)
                with pe.Fori(0, b_out.pairs) as i:
                    tokens_out(b_out, i, o_parts, o_ready, lambda u: u + 1)


_INS = ['x', 'pre_mix_g', 'post_mix_g', 'pre_ffn_g', 'post_ffn_g', 'a_w_in', 'a_v_norm_g', 'a_w_spatial',
        'a_b_spatial', 'a_w_out', 'kv_norm_g', 'w_k', 'w_v', 'b_w_q', 'b_w_o', 'ffn_w_up', 'ffn_conv_w',
        'ffn_conv_b', 'ffn_w_down']


def kernel(**inputs):
    import numpy as np
    import concourse.bacc as bacc
    from concourse.bass_utils import run_bass_kernel_spmd

    nc = bacc.Bacc("TRN2", target_bir_lowering=False, num_devices=1)
    arrays, args = {}, []
    for name in _INS:
        a = np.ascontiguousarray(inputs[name])
        arrays[f"in_{name}"] = a
        args.append(nc.dram_tensor(f"in_{name}", a.shape, mybir.dt.from_np(a.dtype), kind="ExternalInput").ap())
    args.append(nc.dram_tensor("out", arrays["in_x"].shape, F32, kind="ExternalOutput").ap())
    build_trunk(nc, *args)
    r = run_bass_kernel_spmd(nc, [arrays], core_ids=[0])
    return r.results[0]["out"]
```

```python
from contextlib import ExitStack

import concourse.bass as bass
from concourse import mybir

ALU = mybir.AluOpType
ACT = mybir.ActivationFunctionType
AX = mybir.AxisListType
F32 = mybir.dt.float32
F32R = mybir.dt.float32r

P = 128
BLK = 512
UK = 2
RING = 4
EPS = 1e-6
HI, LO = 0, 1
SBUF_START = 16512


class Phase:

    def __init__(self, before, w, starts, step, pairs):
        self.w, self.starts, self.step, self.pairs = w, starts, step, pairs
        self.units = w.shape[0] // (UK * P)
        self.first = before.end if before else 0
        self.block0 = before.block_end if before else 0
        self.end = self.first + 2 * pairs * self.units
        self.block_end = self.block0 + 2 * pairs

    def column(self, i, h):
        return self.starts[h] + i * self.step

    def unit(self, b):
        return self.first + b * self.units


def build_trunk(nc, x, pre_mix_g, post_mix_g, pre_ffn_g, post_ffn_g, a_w_in, a_v_norm_g, a_w_spatial,
                a_b_spatial, a_w_out, kv_norm_g, w_k, w_v, b_w_q, b_w_o, ffn_w_up, ffn_conv_w,
                ffn_conv_b, ffn_w_down, out):
    _, T, D = x.shape
    NH = T // P
    KT = D // P
    G = a_w_spatial.shape[1]
    FF = ffn_w_down.shape[1]
    FT = FF // P
    HEADS = w_k.shape[1] // P
    NB = D // BLK
    TB = BLK // P
    FP = FF // BLK
    TAPS = ffn_conv_w.shape[1]
    PAD = TAPS - 1
    ATT = T + P
    STEPS = HEADS // 2
    LAST = NB - 1
    SCALE = float(P) ** -0.5
    assert T == 2 * P and G == KT and HEADS == KT and a_w_spatial.shape[2] == P

    gate_v = Phase(None, a_w_in[0], (D, D + BLK), 2 * BLK, NB // 2)
    gate_u = Phase(gate_v, a_w_in[0], (0, BLK), 2 * BLK, NB // 2)
    a_out = Phase(gate_u, a_w_out[0], (0, BLK), 2 * BLK, NB // 2)
    up0 = Phase(a_out, ffn_w_up[0], (0, FF), BLK, FP)
    down0 = Phase(up0, ffn_w_down[0], (0, BLK), 2 * BLK, NB // 2)
    q_in = Phase(down0, b_w_q[0], (0, BLK), 2 * BLK, NB // 2)
    k_in = Phase(q_in, w_k, (0, BLK), 2 * BLK, NB // 2)
    v_in = Phase(k_in, w_v, (0, BLK), 2 * BLK, NB // 2)
    b_out = Phase(v_in, b_w_o[0], (0, BLK), 2 * BLK, NB // 2)
    up1 = Phase(b_out, ffn_w_up[1], (0, FF), BLK, FP)
    down1 = Phase(up1, ffn_w_down[1], (0, BLK), 2 * BLK, NB // 2)
    phases = [gate_v, gate_u, a_out, up0, down0, q_in, k_in, v_in, b_out, up1, down1]
    UP, DOWN = (up0, up1), (down0, down1)
    NORMED = (a_out, down0, b_out, down1)
    POST_GAIN = (post_mix_g[0], post_ffn_g[0], post_mix_g[1], post_ffn_g[1])

    at = {"next": SBUF_START}

    def region(nbytes):
        start = at["next"]
        at["next"] += (nbytes + 31) // 32 * 32
        return start

    def place(name, shape, dtype, start):
        return nc.alloc_sbuf_tensor_at(name, [shape[0], *shape[1:]], dtype, offset=start)

    def sb(name, shape, dtype=F32):
        size = 4
        for n in shape[1:]:
            size *= n
        return place(name, shape, dtype, region(size))

    KB = 1024
    h = sb("h", [P, NH, D])
    raw = sb("raw", [P, RING, UK, BLK])
    w_hi = sb("w_hi", [P, RING, UK, BLK], F32R)
    w_lo = sb("w_lo", [P, RING, UK, BLK], F32R)

    x_at = region(32 * KB)
    x_parts = place("x_parts", [P, KT, 2, T], F32R, x_at)
    post_gain = place("post_gain", [P, D], F32, x_at)
    mixed = place("mixed", [P, NB, NH, BLK], F32, x_at + 16 * KB)
    att = place("att", [P, HEADS, ATT], F32, x_at)
    log_beta = place("log_beta", [P, 2, ATT], F32, x_at + 24 * KB)
    att_exp = place("att_exp", [P, 2, ATT], F32, x_at + 27 * KB)

    arena = region(FT * 2 * T * 4)
    u_t = place("u_t", [P, KT, T], F32, arena)
    v_nat = place("v_nat", [P, NH, G, P], F32, arena + 16 * KB)
    mix_parts = place("mix_parts", [P, KT, 2, T], F32R, arena + 32 * KB)
    ws_t = place("ws_t", [P, G, P], F32, arena + 64 * KB)
    v_gain = place("v_gain", [P, D], F32, arena + 72 * KB)
    bias_row = place("bias_row", [1, G, P], F32, arena + 72 * KB)
    v_square = place("v_square", [P, G, P], F32, arena + 80 * KB)
    ws_nat = place("ws_nat", [P, G, P], F32, arena + 32 * KB)
    gain_rows = place("gain_rows", [P, P], F32, arena + 40 * KB)
    conv_rows = place("conv_rows", [P, 2 * (TAPS + 1), P], F32, arena + 41 * KB)
    g_parts = place("g_parts", [P, FT, 2, T], F32R, arena)
    val = place("val", [P, NH, D], F32, arena)
    q_t = place("q_t", [P, HEADS, T], F32, arena + 16 * KB)
    k_t = place("k_t", [P, HEADS, T], F32, arena + 32 * KB)
    kv_parts = place("kv_parts", [P, KT, 2, T], F32R, arena + 48 * KB)
    o_parts = place("o_parts", [P, KT, 2, T], F32R, arena + 16 * KB)

    low = sb("low", [P, TB, T])
    conv_in = sb("conv_in", [P, TB, PAD + T])
    conv_at = region(TB * T * 4)
    conv = place("conv", [P, TB, T], F32, conv_at)
    v_sum = place("v_sum", [P, NH, G], F32, conv_at + KB)
    v_mean = place("v_mean", [P, NH, G], F32, conv_at + KB + 128)
    v_scale = place("v_scale", [P, NH, G], F32, conv_at + KB + 256)
    att_sp = place("att_sp", [P, 2, ATT], F32, conv_at)
    silu_at = region(TB * T * 4)
    silu = place("silu", [P, TB, T], F32, silu_at)
    att_log = place("att_log", [P, 2, ATT], F32, silu_at)
    diag = place("diag", [P, NH, P], F32, conv_at)
    junk = place("junk", [P, NH, BLK], F32, silu_at)

    ident = sb("ident", [P, P])
    later = sb("later", [P, P])
    ones = sb("ones", [P, P])
    row_scale = sb("row_scale", [P, T])
    mask = sb("mask", [P, P])
    NGAIN = 6 * KT
    gains = sb("gains", [P, NGAIN])
    conv_cols = sb("conv_cols", [P, 2, TAPS + 1, 2 * FT])
    half_neg = sb("half_neg", [P, KT * NH])
    block_sq = sb("block_sq", [P, NH, NB])
    post_sum = sb("post_sum", [P, NH])
    post_mean = sb("post_mean", [P, NH])
    post_scale = sb("post_scale", [P, NH])
    stream_sq = sb("stream_sq", [P, NH, NB])
    pre_sum = sb("pre_sum", [P, NH])
    pre_mean = sb("pre_mean", [P, NH])
    pre_scale = sb("pre_scale", [P, NH])
    assert at["next"] <= nc.sbuf_usable_end, at["next"] - nc.sbuf_usable_end

    GAIN_AT = {"mix0": 0, "mix1": KT, "ffn0": 2 * KT, "ffn1": 3 * KT, "kv": 4 * KT}
    PRE_GAIN = (("mix0",), ("ffn0",), ("mix1", "kv"), ("ffn1",))

    with ExitStack() as ctx:
        ps = ctx.enter_context(nc.psum_tensor("ps", [P, 8, BLK], F32))

        def sem(name):
            return ctx.enter_context(nc.semaphore(name))

        x_loaded = [sem(f"x_loaded{i}") for i in range(NH)]
        gains_loaded = sem("gains_loaded")
        taps_loaded = sem("taps_loaded")
        spatial_loaded = sem("spatial_loaded")
        v_gain_loaded = sem("v_gain_loaded")
        bias_loaded = sem("bias_loaded")
        post_gain_loaded = sem("post_gain_loaded")
        constants = sem("constants")
        spatial_masked = sem("spatial_masked")
        gains_turned = sem("gains_turned")
        taps_turned = sem("taps_turned")
        spatial_turned = sem("spatial_turned")
        gains_ready = sem("gains_ready")
        taps_ready = sem("taps_ready")
        ws_ready = sem("ws_ready")
        raw_loaded = [sem(f"raw_loaded{i}") for i in range(RING)]
        unit_hi = sem("unit_hi")
        unit_split = sem("unit_split")
        unit_used = sem("unit_used")
        evacuated = sem("evacuated")
        low_copied = sem("low_copied")
        u_ready = sem("u_ready")
        v_step = sem("v_step")
        v_normed = sem("v_normed")
        group_mixed = sem("group_mixed")
        group_gated = sem("group_gated")
        group_hi = sem("group_hi")
        group_ready = sem("group_ready")
        half_done = sem("half_done")
        squared = sem("squared")
        post_meaned = sem("post_meaned")
        post_scaled = sem("post_scaled")
        h_new = sem("h_new")
        pre_squared = sem("pre_squared")
        pre_meaned = sem("pre_meaned")
        pre_scaled = sem("pre_scaled")
        diag_ready = sem("diag_ready")
        row_spread = sem("row_spread")
        row_ready = sem("row_ready")
        combined = sem("combined")
        x_turned = sem("x_turned")
        x_hi_ready = sem("x_hi_ready")
        x_ready = sem("x_ready")
        conv_step = sem("conv_step")
        silu_ready = sem("silu_ready")
        gated = sem("gated")
        g_hi_ready = sem("g_hi_ready")
        g_ready = sem("g_ready")
        scored = sem("scored")
        att_act = sem("att_act")
        att_dve = sem("att_dve")
        att_ready = sem("att_ready")
        summed = sem("summed")
        weighted = sem("weighted")
        o_hi_ready = sem("o_hi_ready")
        o_ready = sem("o_ready")
        dve_order = sem("dve_order")
        stored = sem("stored")

        def token_bank(ph, h_):
            return 2 * h_ + (4 if ph is a_out else 0)

        def mixing_bank(g2):
            return (g2 + 4) % 8

        def column_bank(h_, flip=0):
            return 4 * ((h_ + flip) % 2)

        def turned(k):
            return ps[:, 4 + k % 4, 0:T]

        SCORES, SUMS, SOFTPLUS, WEIGHTS = 2, 4, 6, 8

        V_UNITS = NB * v_in.units
        WEIGHTED = [27, 27, 28, 28, 31, 31, 34, 34]
        OUT_SLOT = [32, 32, 33, 33, 35, 35, 38, 38]

        def weighted_bank(j):
            return 4 + j % 4

        def step_at(n, offset):
            j = (n - offset) // 3
            return j if (n - offset) % 3 == 0 and 0 <= j < STEPS else None

        block = ctx.enter_context(nc.Block())

        @block.sync
        def _(sp):
            def load_pair(ph, i, fresh=False):
                for hb in range(2):
                    for u in range(ph.units):
                        k = hb * ph.units + u
                        if not (fresh and k < RING):
                            sp.wait_ge(unit_split, i * (2 * ph.units) + (ph.first + k - RING + 1))
                        rows = ph.w[u * UK * P:(u + 1) * UK * P, bass.ds(ph.column(i, hb), BLK)]
                        sp.dma_start(raw[:, k % RING, :, :],
                                     rows.rearrange("(k p) n -> p k n", p=P)).then_inc(raw_loaded[k % RING], 16)

            for half in range(NH):
                sp.dma_start(h[:, half, :], x[0, half * P:(half + 1) * P, :]).then_inc(x_loaded[half], 16)
            for ph in phases:
                if ph is gate_v:
                    load_pair(ph, 0, fresh=True)
                with sp.Fori(1 if ph is gate_v else 0, ph.pairs) as i:
                    load_pair(ph, i)
            for c in range(NB):
                for half in range(NH):
                    sp.wait_ge(h_new, NH * NB * (len(NORMED) - 1) + NH * c + half + 1)
                    sp.dma_start(out[0, half * P:(half + 1) * P, c * BLK:(c + 1) * BLK],
                                 h[:, half, c * BLK:(c + 1) * BLK]).then_inc(stored, 16)
            sp.wait_ge(stored, 16 * NH * NB)

        @block.gpsimd
        def _(pool):
            pool.memset(half_neg[:, :], -0.5).then_inc(constants, 1)
            pool.memset(ident[:, :], 0.0).then_inc(constants, 1)
            pool.memset(ones[:, :], 1.0).then_inc(constants, 1)
            pool.memset(mask[:, :], 1.0).then_inc(constants, 1)
            pool.wait_ge(constants, 4)
            pool.affine_select(out=ident[:, :], in_=ident[:, :], compare_op=ALU.not_equal, fill=1.0,
                               base=0, pattern=[[-1, P]], channel_multiplier=1).then_inc(constants, 1)
            pool.affine_select(out=later[:, :], in_=ones[:, :], compare_op=ALU.is_gt, fill=0.0,
                               base=0, pattern=[[-1, P]], channel_multiplier=1).then_inc(constants, 1)
            pool.affine_select(out=mask[:, :], in_=mask[:, :], compare_op=ALU.is_gt, fill=0.0,
                               base=0, pattern=[[1, P]], channel_multiplier=-1).then_inc(constants, 1)

            def rsqrt(to, of, n, ready, done, count):
                pool.wait_ge(ready, count)
                pool.tensor_tensor(to, of, half_neg[:, 0:n], ALU.pow).then_inc(done, 1)

            def pre_rsqrt(t):
                rsqrt(pre_scale[:, :], pre_mean[:, :], NH, pre_meaned, pre_scaled, t + 1)

            def load_post_gain(s):
                pool.dma_start(post_gain[:, :], POST_GAIN[s].unsqueeze(0).to_broadcast([P, D])
                               ).then_inc(post_gain_loaded, 16)

            pool.dma_start(ws_nat[:, :, :], a_w_spatial[0].rearrange("g t s -> t g s")).then_inc(spatial_loaded, 16)
            for layer in range(2):
                row = layer * (TAPS + 1)
                pool.dma_start(conv_rows[0:2 * FT, row:row + TAPS, :], ffn_conv_w[layer].rearrange("t (f p) -> f t p", p=P)
                               ).then_inc(taps_loaded, 16)
                pool.dma_start(conv_rows[0:2 * FT, row + TAPS, :], ffn_conv_b[layer].rearrange("(f p) -> f p", p=P)
                               ).then_inc(taps_loaded, 16)
            pool.dma_start(v_gain[:, :], a_v_norm_g[0:1, :].to_broadcast([P, D])).then_inc(v_gain_loaded, 16)
            pre_rsqrt(0)
            pool.wait_ge(spatial_loaded, 16)
            pool.affine_select(out=ws_nat[:, :, :], in_=ws_nat[:, :, :], compare_op=ALU.is_ge, fill=0.0,
                               base=0, pattern=[[0, G], [-1, P]], channel_multiplier=1).then_inc(spatial_masked, 1)
            rsqrt(v_scale[:, :, :].rearrange("p a g -> p (a g)"), v_mean[:, :, :].rearrange("p a g -> p (a g)"),
                  NH * G, v_step, v_step, 5)
            for half in range(NH):
                pool.wait_ge(v_step, 7 + half)
                if half == 0:
                    pool.wait_ge(v_gain_loaded, 16)
                vh = v_nat[:, half, :, :].rearrange("p g d -> p (g d)")
                pool.tensor_tensor(vh, vh, v_gain[:, :], ALU.mult).then_inc(v_normed, 1)
            pool.wait_ge(v_normed, NH)
            pool.dma_start(bias_row[:, :, :], a_b_spatial).then_inc(bias_loaded, 16)
            for s, ph in enumerate(NORMED):
                if s == 2:
                    for j in range(STEPS):
                        pool.wait_ge(att_act, 4 * j + 4)
                        for c in (0, T):
                            heads = att[:, 2 * j:2 * j + 2, c:c + P]
                            last = pool.affine_select(out=heads, in_=heads, compare_op=ALU.is_gt, fill=0.0, base=0,
                                                      pattern=[[0, 2], [1, P]], channel_multiplier=-1)
                        last.then_inc(att_ready, 1)
                    pool.wait_ge(weighted, STEPS)
                else:
                    pool.wait_ge(unit_used, ph.first)
                load_post_gain(s)
                for half in range(NH):
                    rsqrt(post_scale[:, half:half + 1], post_mean[:, half:half + 1], 1,
                          post_meaned, post_scaled, NH * s + half + 1)
                if s + 1 < len(NORMED):
                    pre_rsqrt(s + 1)

        @block.scalar
        def _(act):
            def units(base, a, b):
                for k in range(a, b):
                    slot = k % RING
                    if isinstance(base, int):
                        act.wait_ge(raw_loaded[slot], 16 * ((base + k) // RING + 1))
                    else:
                        act.wait_ge(raw_loaded[slot], base_loads[0] + 16 * (k // RING + 1))
                    if not isinstance(base, int) or base + k >= RING:
                        act.wait_ge(unit_used, base + (k - RING + 1))
                    act.copy(w_hi[:, slot, :, :], raw[:, slot, :, :]).then_inc(unit_hi, 1)

            base_loads = [None]

            def copy_low(ph, block_no, low_no, used, bank, scale=None):
                act.wait_ge(unit_used, used)
                act.wait_ge(evacuated, block_no)
                src = ps[:, bank:bank + TB, T:2 * T]
                ins = act.copy(low[:, :, :], src) if scale is None else act.mul(low[:, :, :], src, scale)
                ins.then_inc(low_copied, 1)

            def square(s, b):
                ph = NORMED[s]
                bank = token_bank(ph, b % 2)
                if s + b:
                    act.wait_ge(squared, NH * (NB * s + b))
                for half in range(NH):
                    if half == 0:
                        act.wait_ge(half_done, NB * s + b + 1)
                    else:
                        act.wait_ge(unit_used, ph.unit(b + 1))
                    act.activation(junk[:, half, :], ps[:, bank + half, :], ACT.Square,
                                   accum_out=block_sq[:, half, b:b + 1]).then_inc(squared, 1)

            def square_stream(t, c):
                if t:
                    act.wait_ge(h_new, NH * (NB * (t - 1) + c + 1))
                    act.wait_ge(squared, NH * NB * t)
                if t + c:
                    act.wait_ge(pre_squared, NB * t + c)
                for half in range(NH):
                    if t == 0:
                        act.wait_ge(x_loaded[half], 16)
                    last = act.activation(junk[:, half, :], h[:, half, c * BLK:(c + 1) * BLK], ACT.Square,
                                          accum_out=stream_sq[:, half, c:c + 1])
                last.then_inc(pre_squared, 1)

            def x_high(t, tiles):
                for k in tiles:
                    act.wait_ge(x_turned, KT * t + k + 1)
                    for name in PRE_GAIN[t]:
                        to = kv_parts if name == "kv" else x_parts
                        c = GAIN_AT[name] + k
                        ins = act.activation(to[:, k, HI, :], turned(k), ACT.Copy, scale=gains[:, c:c + 1])
                    ins.then_inc(x_hi_ready, 1)

            for row, g in ((0, pre_mix_g), (2 * KT, pre_ffn_g)):
                act.dma_start(gain_rows[row:row + 2 * KT, :], g.rearrange("l (k p) -> (l k) p", p=P)
                              ).then_inc(gains_loaded, 16)
            act.dma_start(gain_rows[4 * KT:5 * KT, :], kv_norm_g.rearrange("(k p) -> k p", p=P)).then_inc(gains_loaded, 16)
            act.dma_start(gain_rows[5 * KT:6 * KT, :], a_v_norm_g[0].rearrange("(k p) -> k p", p=P)
                          ).then_inc(gains_loaded, 16)
            def turn_and_split(t, ph):
                x_high(t, range(0, TB))
                square_stream(t, 0)
                units(ph.first, RING - 1, RING)
                for c in (1, 2):
                    x_high(t, range(c * TB, (c + 1) * TB))
                    square_stream(t, c)
                square_stream(t, NB - 1)
                units(ph.first, RING, RING + 2)
                x_high(t, range((NB - 1) * TB, KT))
                units(ph.first, RING + 2, ph.units)

            units(0, 0, RING - 1)
            act.wait_ge(gains_ready, 1)
            turn_and_split(0, gate_v)

            def gelu_v(b):
                act.wait_ge(unit_used, gate_v.unit(b + 1))
                act.wait_ge(pre_scaled, 1)
                bank = token_bank(gate_v, b % 2)
                for half in range(NH):
                    last = act.activation(v_nat[:, half, b * TB:(b + 1) * TB, :].rearrange("p g d -> p (g d)"),
                                          ps[:, bank + half, :], ACT.Gelu_apprx_tanh,
                                          scale=pre_scale[:, half:half + 1])
                last.then_inc(evacuated, 1)

            def gelu_u(b):
                act.wait_ge(combined, b + 1)
                tiles = u_t[:, b * TB:(b + 1) * TB, :]
                act.activation(tiles, tiles, ACT.Gelu_apprx_tanh).then_inc(u_ready, 1)

            U = gate_v.units
            for b in range(1, NB):
                units(gate_v.unit(b), 0, RING)
                gelu_v(b - 1)
                if b == 2:
                    act.wait_ge(spatial_turned, 1)
                    act.copy(ws_t[:, :, :].rearrange("p (b g) s -> p b (g s)", b=4), ps[:, 4:8, :]
                             ).then_inc(ws_ready, 1)
                units(gate_v.unit(b), RING, U)
            for b in range(NB):
                units(gate_u.unit(b), 0, RING)
                if b == 0:
                    gelu_v(LAST)
                    units(gate_u.unit(b), RING, U)
                else:
                    copy_low(gate_u, gate_u.block0 + b - 1, b, gate_u.unit(b), column_bank(b - 1, 1))
                    units(gate_u.unit(b), RING, RING + 2)
                    gelu_u(b - 1)
                    units(gate_u.unit(b), RING + 2, U)

            def group_high(g2):
                act.wait_ge(group_gated, g2 + 1)
                act.copy(mix_parts[:, 2 * g2:2 * g2 + 2, HI, :], v_square[:, :, :].rearrange(
                    "p g d -> p (g d)")[:, (g2 % 4) * 2 * T:(g2 % 4 + 1) * 2 * T].rearrange("p (g t) -> p g t", g=2)
                         ).then_inc(group_hi, 1)

            units(a_out.first, 0, RING - 1)
            copy_low(gate_u, gate_u.block_end - 1, NB, gate_u.end, column_bank(LAST % 2, 1))
            for g2 in range(2):
                group_high(g2)
            units(a_out.first, RING - 1, RING)
            gelu_u(LAST)
            for g2 in range(2, 4):
                group_high(g2)
            for g2 in range(4, 8):
                units(a_out.first, g2, g2 + 1)
                group_high(g2)
            for b in range(1, NB):
                units(a_out.unit(b), 0, RING)
                square(0, b - 1)
                units(a_out.unit(b), RING, U)

            def after_normed(s, nxt):
                units(nxt.first, 0, RING - 1)
                square(s, LAST)
                turn_and_split(s + 1, nxt)

            def ffn_gate_silu(ff_block, j):
                act.wait_ge(conv_step, 3 * ff_block + 3)
                if not isinstance(j, int) or j:
                    act.wait_ge(gated, j)
                act.activation(silu[:, :, :], conv[:, :, :], ACT.Silu).then_inc(silu_ready, 1)

            def ffn_high(layer, i):
                act.wait_ge(gated, i + layer * FP + 1)
                act.copy(g_parts[:, bass.ds(i * TB, TB), HI, :], conv[:, :, :]).then_inc(g_hi_ready, 1)

            def ffn_up(layer, s):
                ph = UP[layer]
                low0 = 4 + 8 * layer + 2 * FP * layer

                def gate_part(i):
                    base = i * (2 * U) + ph.first
                    units(base, U, U + RING)
                    copy_low(ph, i * 2 + ph.block0, None, base + U, column_bank(0))
                    units(base, U + RING, 2 * U)
                    ffn_gate_silu(i * 2 + 2 * FP * layer, i + FP * layer)

                def value_part(i, base, last):
                    copy_low(ph, i * 2 + (ph.block0 + 1), None, i * (2 * U) + (ph.first + 2 * U), column_bank(1))
                    units(base, RING, last - 1)
                    ffn_high(layer, i)
                    units(base, last - 1, last)

                after_normed(s, ph)
                gate_part(0)
                with act.Fori(1, ph.pairs) as i:
                    base = i * (2 * U) + ph.first
                    base_loads[0] = i * (16 * 2 * U // RING) + 16 * ph.first // RING
                    units(base, 0, RING)
                    copy_low(ph, i * 2 + (ph.block0 - 1), None, base, column_bank(1))
                    units(base, RING, U - 1)
                    ffn_high(layer, i - 1)
                    units(base, U - 1, U)
                    gate_part(i)

            def ffn_down(layer, s):
                ph, up = DOWN[layer], UP[layer]
                units(ph.first, 0, RING)
                copy_low(up, up.block_end - 1, None, up.end, column_bank(1))
                units(ph.first, RING, U - 1)
                ffn_high(layer, FP - 1)
                units(ph.first, U - 1, ph.units)
                for b in range(1, NB):
                    units_of(ph, b, 0, RING)
                    square(s, b - 1)
                    units_of(ph, b, RING, ph.units)

            def units_of(ph, b, a, e):
                units(ph.first, b * ph.units + a, b * ph.units + e)

            ffn_up(0, 0)
            ffn_down(0, 1)

            after_normed(1, q_in)
            for ph in (q_in, k_in):
                for b in range(NB):
                    if ph is q_in and b == 0:
                        continue
                    units(ph.unit(b), 0, RING)
                    done, bank = ph.block0 + b - 1, column_bank((b + 1) % 2)
                    scaled = (ph is q_in) or b == 0
                    copy_low(ph, done, None, ph.unit(b), bank, SCALE if scaled else None)
                    units(ph.unit(b), RING, U)

            def copy_value(b):
                act.wait_ge(unit_used, v_in.unit(b + 1))
                bank = token_bank(v_in, b % 2)
                for half in range(NH):
                    last = act.activation(val[:, half, b * BLK:(b + 1) * BLK], ps[:, bank + half, :], ACT.Copy,
                                          scale=pre_scale[:, half:half + 1])
                last.then_inc(evacuated, 1)

            def att_softplus_log(j):
                act.wait_ge(scored, j + 1)
                if j:
                    act.wait_ge(att_dve, 4 * (j - 1) + 3)
                act.activation(att_log[:, :, :], ps[:, 4:6, 0:ATT], ACT.Abs).then_inc(att_act, 1)
                act.wait_ge(att_act, 4 * j + 1)
                act.activation(att_log[:, :, :], att_log[:, :, :], ACT.Exp, scale=-1.0).then_inc(att_act, 1)
                act.wait_ge(att_act, 4 * j + 2)
                act.activation(att_log[:, :, :], att_log[:, :, :], ACT.Ln, bias=1.0).then_inc(att_act, 1)

            def att_weight(j):
                act.wait_ge(att_dve, 4 * j + 4)
                act.activation(att[:, 2 * j:2 * j + 2, :], att_exp[:, :, :], ACT.Exp).then_inc(att_act, 1)

            def out_high(j):
                act.wait_ge(weighted, j + 1)
                act.copy(o_parts[:, 2 * j:2 * j + 2, HI, :], ps[:, weighted_bank(j), :].rearrange("p (a t) -> p a t", a=2)
                         ).then_inc(o_hi_ready, 1)

            act.preload_act_table_set("natural_log_exp_and_others")
            for n in range(V_UNITS + b_out.units):
                units(v_in.first, n, n + 1)
                if n == RING - 1:
                    copy_low(k_in, k_in.block_end - 1, None, k_in.end, column_bank(1))
                if (n - RING + 1) % U == 0 and 0 < (n - RING + 1) // U <= NB:
                    copy_value((n - RING + 1) // U - 1)
                j = step_at(n, WEIGHTS)
                if j is not None:
                    att_weight(j)
                j = step_at(n, SOFTPLUS)
                if j is not None:
                    att_softplus_log(j)
                for j in range(STEPS):
                    if n == OUT_SLOT[j]:
                        out_high(j)
            for b in range(1, NB):
                units(b_out.unit(b), 0, RING)
                square(2, b - 1)
                units(b_out.unit(b), RING, U)

            ffn_up(1, 2)
            ffn_down(1, 3)
            square(3, LAST)

        @block.vector
        def _(dve):
            def units(base, a, b):
                for k in range(a, b):
                    slot = k % RING
                    dve.wait_ge(unit_hi, base + (k + 1))
                    dve.tensor_tensor(w_lo[:, slot, :, :], raw[:, slot, :, :], w_hi[:, slot, :, :].bitcast(F32),
                                      ALU.subtract).then_inc(unit_split, 1)

            ordered = [0]

            def link(ins):
                ordered[0] += 1
                ins.then_inc(dve_order, 1)
                dve.wait_ge(dve_order, ordered[0])

            def add_low(to, low_no, bank, scale=None):
                dve.wait_ge(low_copied, low_no)
                src = ps[:, bank:bank + TB, 0:T]
                if scale is None:
                    dve.tensor_tensor(to, src, low[:, :, :], ALU.add).then_inc(evacuated, 1)
                else:
                    dve.scalar_tensor_tensor(out=to, in0=src, scalar=scale, in1=low[:, :, :],
                                             op0=ALU.mult, op1=ALU.add).then_inc(evacuated, 1)

            def scale_tokens(to, block_no, low_no):
                dve.wait_ge(evacuated, block_no + 1)
                dve.tensor_tensor(to, to, row_scale[:, :].unsqueeze(1).to_broadcast([P, TB, T]), ALU.mult
                                  ).then_inc(combined, 1)

            def gain_block(s, b):
                dve.wait_ge(post_gain_loaded, 16 * (s + 1))
                bank = token_bank(NORMED[s], b % 2)
                for half in range(NH):
                    dve.wait_ge(squared, NH * (NB * s + b) + half + 1)
                    last = dve.tensor_tensor(mixed[:, b, half, :], ps[:, bank + half, :],
                                             post_gain[:, b * BLK:(b + 1) * BLK], ALU.mult)
                last.then_inc(evacuated, 1)

            def post_norm(s):
                for half in range(NH):
                    dve.wait_ge(squared, NH * (NB * s + LAST) + half + 1)
                    link(dve.tensor_reduce(post_sum[:, half:half + 1], block_sq[:, half, :], AX.X, ALU.add))
                    dve.tensor_scalar(post_mean[:, half:half + 1], post_sum[:, half:half + 1], 1.0 / D, EPS,
                                      ALU.mult, ALU.add).then_inc(post_meaned, 1)
                gain_block(s, LAST)

            def update_stream(s, c):
                for half in range(NH):
                    if c == 0:
                        dve.wait_ge(post_scaled, NH * s + half + 1)
                        dve.wait_ge(evacuated, NORMED[s].block_end)
                    hc = h[:, half, c * BLK:(c + 1) * BLK]
                    dve.scalar_tensor_tensor(out=hc, in0=mixed[:, c, half, :],
                                             scalar=post_scale[:, half:half + 1], in1=hc,
                                             op0=ALU.mult, op1=ALU.add).then_inc(h_new, 1)

            def pre_means(t):
                dve.wait_ge(pre_squared, NB * (t + 1))
                link(dve.tensor_reduce(pre_sum[:, :], stream_sq[:, :, :], AX.X, ALU.add))
                dve.tensor_scalar(pre_mean[:, :], pre_sum[:, :], 1.0 / D, EPS, ALU.mult, ALU.add
                                  ).then_inc(pre_meaned, 1)

            def pre_diagonals(t):
                dve.wait_ge(pre_scaled, t + 1)
                for half in range(NH):
                    last = dve.tensor_scalar(diag[:, half, :], ident[:, :], pre_scale[:, half:half + 1], None, ALU.mult)
                last.then_inc(diag_ready, 1)

            def turn_and_split(t, ph):
                if t:
                    update_stream(t - 1, 0)
                x_low(t, range(0, TB))
                if t:
                    update_stream(t - 1, 1)
                units(ph.first, RING - 1, RING)
                x_low(t, range(TB, 2 * TB))
                if t:
                    update_stream(t - 1, 2)
                    update_stream(t - 1, 3)
                x_low(t, range(2 * TB, 3 * TB))
                units(ph.first, RING, RING + 2)
                pre_means(t)
                x_low(t, range(3 * TB, KT))
                pre_diagonals(t)
                units(ph.first, RING + 2, ph.units)

            def copy_row_scale(t):
                dve.wait_ge(row_spread, t + 1)
                dve.tensor_copy(row_scale[:, :], ps[:, 4, 0:T]).then_inc(row_ready, 1)

            def x_low(t, tiles):
                for k in tiles:
                    dve.wait_ge(x_hi_ready, KT * t + k + 1)
                    for name in PRE_GAIN[t]:
                        to = kv_parts if name == "kv" else x_parts
                        c = GAIN_AT[name] + k
                        ins = dve.scalar_tensor_tensor(out=to[:, k, LO, :], in0=turned(k), scalar=gains[:, c:c + 1],
                                                       in1=to[:, k, HI, :].bitcast(F32),
                                                       op0=ALU.mult, op1=ALU.subtract)
                    ins.then_inc(x_ready, 1)

            link(dve.memset(conv_in[:, :, 0:PAD], 0.0))
            dve.wait_ge(gains_turned, 1)
            dve.tensor_copy(gains[:, :], ps[:, 3, 0:NGAIN]).then_inc(gains_ready, 1)
            units(0, 0, RING - 1)
            dve.wait_ge(gains_ready, 1)
            turn_and_split(0, gate_v)
            U = gate_v.units
            units(gate_v.unit(1), 0, 3)
            copy_row_scale(0)
            units(gate_v.unit(1), 3, U)
            units(gate_v.unit(2), 0, U)
            units(gate_v.unit(3), 0, RING)
            dve.wait_ge(taps_turned, 1)
            dve.tensor_copy(conv_cols[:, :, :, :].rearrange("p l t f -> p l (t f)"),
                            ps[:, 4:6, 0:(TAPS + 1) * 2 * FT]).then_inc(taps_ready, 1)
            units(gate_v.unit(3), RING, U)

            def square_v(half):
                if half == 0:
                    dve.wait_ge(evacuated, gate_v.block_end)
                dve.tensor_tensor(v_square[:, :, :], v_nat[:, half, :, :], v_nat[:, half, :, :], ALU.mult
                                  ).then_inc(v_step, 1)

            def sum_v(half):
                dve.wait_ge(v_step, 2 * half + 1)
                dve.tensor_reduce(v_sum[:, half, :], v_square[:, :, :], AX.X, ALU.add).then_inc(v_step, 1)

            def mean_v():
                dve.wait_ge(v_step, 4)
                dve.tensor_scalar(v_mean[:, :, :], v_sum[:, :, :], 1.0 / P, EPS, ALU.mult, ALU.add
                                  ).then_inc(v_step, 1)

            def norm_v(half):
                dve.wait_ge(v_step, 6)
                dve.tensor_tensor(v_nat[:, half, :, :], v_nat[:, half, :, :],
                                  v_scale[:, half, :].unsqueeze(2).to_broadcast([P, G, P]), ALU.mult
                                  ).then_inc(v_step, 1)

            def u_block(b):
                return u_t[:, b * TB:(b + 1) * TB, :]

            def add_u(b):
                add_low(u_block(b), b + 1, column_bank(b % 2, 1))
                scale_tokens(u_block(b), gate_u.block0 + b, b + 1)

            units(gate_u.unit(0), 0, RING)
            square_v(0)
            units(gate_u.unit(0), RING, RING + 1)
            sum_v(0)
            units(gate_u.unit(0), RING + 1, RING + 2)
            dve.wait_ge(v_step, 2)
            square_v(1)
            units(gate_u.unit(0), RING + 2, RING + 3)
            sum_v(1)
            units(gate_u.unit(0), RING + 3, U)
            mean_v()
            units(gate_u.unit(1), 0, RING)
            add_u(0)
            units(gate_u.unit(1), RING, RING + 1)
            norm_v(0)
            units(gate_u.unit(1), RING + 1, RING + 3)
            norm_v(1)
            units(gate_u.unit(1), RING + 3, U)
            for b in range(2, NB):
                units(gate_u.unit(b), 0, RING)
                add_u(b - 1)
                units(gate_u.unit(b), RING, U)

            def gate_place(g2):
                return v_square[:, :, :].rearrange("p g d -> p (g d)")[:, (g2 % 4) * 2 * T:(g2 % 4 + 1) * 2 * T]

            def gate_group(g2):
                dve.wait_ge(group_mixed, g2 + 1)
                dve.wait_ge(u_ready, g2 // 2 + 1)
                dve.tensor_tensor(gate_place(g2), ps[:, mixing_bank(g2), :],
                                  u_t[:, 2 * g2:2 * g2 + 2, :].rearrange("p g t -> p (g t)"), ALU.mult
                                  ).then_inc(group_gated, 1)

            def group_low(g2):
                dve.wait_ge(group_hi, g2 + 1)
                dve.tensor_tensor(mix_parts[:, 2 * g2:2 * g2 + 2, LO, :],
                                  gate_place(g2).rearrange("p (g t) -> p g t", g=2),
                                  mix_parts[:, 2 * g2:2 * g2 + 2, HI, :].bitcast(F32), ALU.subtract
                                  ).then_inc(group_ready, 1)

            units(a_out.first, 0, RING - 1)
            gate_group(0)
            gate_group(1)
            add_low(u_block(LAST), LAST + 1, column_bank(LAST % 2, 1))
            group_low(0)
            scale_tokens(u_block(LAST), gate_u.block0 + LAST, LAST + 1)
            group_low(1)
            units(a_out.first, RING - 1, RING)
            gate_group(2)
            gate_group(3)
            group_low(2)
            group_low(3)
            for g2 in range(4, 8):
                gate_group(g2)
                units(a_out.first, g2, g2 + 1)
                group_low(g2)
            for b in range(1, NB):
                units(a_out.unit(b), 0, RING)
                gain_block(0, b - 1)
                units(a_out.unit(b), RING, U)

            def after_normed(s, nxt):
                units(nxt.first, 0, RING - 1)
                post_norm(s)
                turn_and_split(s + 1, nxt)

            def ffn_taps(layer, i, part, tap, ff_block):
                for m in range(TB):
                    tile = i * TB + (part * FT + m)
                    w = conv_cols[:, layer, tap, bass.ds(tile, 1)]
                    src = conv_in[:, m, tap:tap + T]
                    if tap == PAD:
                        ins = dve.tensor_scalar(conv[:, m, :], src, w, conv_cols[:, layer, TAPS, bass.ds(tile, 1)],
                                                ALU.mult, ALU.add)
                    else:
                        ins = dve.scalar_tensor_tensor(out=conv[:, m, :], in0=src, scalar=w, in1=conv[:, m, :],
                                                       op0=ALU.mult, op1=ALU.add)
                ins.then_inc(conv_step, 1)

            def ffn_block(layer, i, part, base, a, e):
                ff = i * 2 + (2 * FP * layer + part)
                low_no = i * 2 + (2 * FP * layer + part + NB + 2 * NB * layer + 1)
                add_low(conv_in[:, :, PAD:PAD + T], low_no, column_bank(part))
                scale_tokens(conv_in[:, :, PAD:PAD + T], i * 2 + (UP[layer].block0 + part), low_no)
                units(base, a + RING, a + RING + 1)
                dve.wait_ge(combined, low_no)
                if part:
                    dve.wait_ge(silu_ready, i + (layer * FP + 1))
                ffn_taps(layer, i, part, 2, ff)
                units(base, a + RING + 1, a + RING + 2)
                dve.wait_ge(conv_step, ff * 3 + 1)
                ffn_taps(layer, i, part, 1, ff)
                units(base, a + RING + 2, a + RING + 3)
                dve.wait_ge(conv_step, ff * 3 + 2)
                ffn_taps(layer, i, part, 0, ff)
                if part:
                    dve.wait_ge(conv_step, ff * 3 + 3)
                    dve.tensor_tensor(conv[:, :, :], conv[:, :, :], silu[:, :, :], ALU.mult).then_inc(gated, 1)
                units(base, a + RING + 3, e)
                if part:
                    dve.wait_ge(g_hi_ready, i + (layer * FP + 1))
                    dve.tensor_tensor(g_parts[:, bass.ds(i * TB, TB), LO, :], conv[:, :, :],
                                      g_parts[:, bass.ds(i * TB, TB), HI, :].bitcast(F32), ALU.subtract
                                      ).then_inc(g_ready, 1)

            def ffn_up(layer, s):
                ph = UP[layer]
                after_normed(s, ph)
                units(ph.first, U, U + 3)
                copy_row_scale(s + 1)
                units(ph.first, U + 3, U + RING)
                ffn_block(layer, 0, 0, ph.first, U, 2 * U)
                with dve.Fori(1, ph.pairs) as i:
                    base = i * (2 * U) + ph.first
                    units(base, 0, RING)
                    ffn_block(layer, i - 1, 1, base, 0, U)
                    units(base, U, U + RING)
                    ffn_block(layer, i, 0, base, U, 2 * U)

            def ffn_down(layer, s):
                ph = DOWN[layer]
                units(ph.first, 0, RING)
                ffn_block(layer, FP - 1, 1, ph.first, 0, U)
                units(ph.first, U, ph.units)
                for b in range(1, NB):
                    k = b * ph.units
                    units(ph.first, k, k + RING)
                    gain_block(s, b - 1)
                    units(ph.first, k + RING, k + ph.units)

            ffn_up(0, 0)
            ffn_down(0, 1)

            after_normed(1, q_in)
            low_no = NB + 2 * FP
            for ph in (q_in, k_in):
                for b in range(NB):
                    if ph is q_in and b == 0:
                        continue
                    units(ph.unit(b), 0, 3)
                    if low_no == NB + 2 * FP:
                        copy_row_scale(2)
                    units(ph.unit(b), 3, RING)
                    low_no += 1
                    to, c = (q_t, (b - 1) % NB) if (ph is q_in or b == 0) else (k_t, b - 1)
                    to_block = to[:, c * TB:(c + 1) * TB, :]
                    add_low(to_block, low_no, column_bank((b + 1) % 2), SCALE if to is q_t else None)
                    scale_tokens(to_block, ph.block0 + b - 1, low_no)
                    units(ph.unit(b), RING, U)

            def att_softplus(j):
                dve.wait_ge(att_act, 4 * j + 3)
                if j:
                    dve.wait_ge(summed, j)
                dve.scalar_tensor_tensor(out=att_sp[:, :, :], in0=ps[:, 4:6, 0:ATT], scalar=0.0, in1=att_log[:, :, :],
                                         op0=ALU.max, op1=ALU.add).then_inc(att_dve, 1)
                dve.wait_ge(att_dve, 4 * j + 1)
                for c in (0, T):
                    last = dve.tensor_tensor(att_sp[:, :, c:c + P], att_sp[:, :, c:c + P],
                                             mask[:, :].unsqueeze(1).to_broadcast([P, 2, P]), ALU.mult)
                last.then_inc(att_dve, 1)
                dve.scalar_tensor_tensor(out=log_beta[:, :, :], in0=ps[:, 4:6, 0:ATT], scalar=0.0,
                                         in1=att_log[:, :, :], op0=ALU.min, op1=ALU.subtract).then_inc(att_dve, 1)

            def att_exponent(j):
                dve.wait_ge(summed, j + 1)
                dve.wait_ge(att_dve, 4 * j + 3)
                dve.tensor_tensor(att_exp[:, :, :], log_beta[:, :, :], ps[:, 6:8, 0:ATT], ALU.subtract
                                  ).then_inc(att_dve, 1)

            def out_low(j):
                dve.wait_ge(o_hi_ready, j + 1)
                dve.tensor_tensor(o_parts[:, 2 * j:2 * j + 2, LO, :],
                                  ps[:, weighted_bank(j), :].rearrange("p (a t) -> p a t", a=2),
                                  o_parts[:, 2 * j:2 * j + 2, HI, :].bitcast(F32), ALU.subtract).then_inc(o_ready, 1)

            for n in range(V_UNITS + b_out.units):
                units(v_in.first, n, n + 1)
                if n == RING - 1:
                    add_low(k_t[:, LAST * TB:(LAST + 1) * TB, :], low_no + 1, column_bank(1))
                    scale_tokens(k_t[:, LAST * TB:(LAST + 1) * TB, :], k_in.block_end - 1, low_no + 1)
                j = step_at(n, WEIGHTS)
                if j is not None:
                    att_exponent(j)
                j = step_at(n, SOFTPLUS)
                if j is not None:
                    att_softplus(j)
                for j in range(STEPS):
                    if n == OUT_SLOT[j]:
                        out_low(j)
            for b in range(1, NB):
                units(b_out.unit(b), 0, RING)
                gain_block(2, b - 1)
                units(b_out.unit(b), RING, U)

            ffn_up(1, 2)
            ffn_down(1, 3)
            post_norm(3)
            for c in range(NB):
                update_stream(3, c)

        @block.tensor
        def _(pe):
            U = gate_v.units

            def columns_out(ph, i, src, ready, first_ready, flip=0, t=None):
                for hb in range(2):
                    bank = column_bank(hb, flip)
                    for u in range(ph.units):
                        k = hb * ph.units + u
                        slot = k % RING
                        pe.wait_ge(unit_split, i * (2 * ph.units) + (ph.first + k + 1))
                        pe.wait_ge(ready, first_ready + UK * u + UK)
                        if u == 0:
                            pe.wait_ge(evacuated, i * 2 + (ph.block0 + hb - 1))
                            if t is not None and hb:
                                pe.wait_ge(row_ready, t + 1)
                        for m in range(TB):
                            for kk in range(UK):
                                kt = UK * u + kk
                                first, last = kt == 0, kt == KT - 1
                                pe.matmul(ps[:, bank + m, :], w_hi[:, slot, kk, m * P:(m + 1) * P],
                                          src[:, kt, :, :].rearrange("p a t -> p (a t)"), start=first, stop=False,
                                          skip_group_check=True)
                                mm = pe.matmul(ps[:, bank + m, 0:T], w_lo[:, slot, kk, m * P:(m + 1) * P],
                                               src[:, kt, HI, :], start=False, stop=last, skip_group_check=True)
                        mm.then_inc(unit_used, 1)
                        if t is not None and hb == 0:
                            turn_rest(t, u)

            def tokens_out_unit(ph, i, hb, u, src, bank):
                k = hb * ph.units + u
                slot = k % RING
                for half in range(NH):
                    t0 = half * P
                    for kk in range(UK):
                        kt = UK * u + kk
                        first, last = kt == 0, kt == UK * ph.units - 1
                        to = ps[:, bank + half, :]
                        pe.matmul(to, src[:, kt, HI, t0:t0 + P], w_hi[:, slot, kk, :], start=first, stop=False)
                        pe.matmul(to, src[:, kt, HI, t0:t0 + P], w_lo[:, slot, kk, :], start=False, stop=False)
                        mm = pe.matmul(to, src[:, kt, LO, t0:t0 + P], w_hi[:, slot, kk, :], start=False, stop=last)
                    if half == 0 and last and ph in NORMED:
                        mm.then_inc(half_done, 1)
                mm.then_inc(unit_used, 1)

            def tokens_out(ph, i, src, ready, count, t=None):
                for hb in range(2):
                    tokens_out_block(ph, i, hb, src, ready, count, t if hb == 0 else None)

            def tokens_out_block(ph, i, hb, src, ready, count, t=None):
                for u in range(ph.units):
                    pe.wait_ge(unit_split, i * (2 * ph.units) + (ph.first + hb * ph.units + u + 1))
                    pe.wait_ge(ready, count(u))
                    if u == 0 and not (ph is gate_v and isinstance(i, int) and i == 0):
                        pe.wait_ge(evacuated, i * 2 + (ph.block0 + hb - 1))
                    tokens_out_unit(ph, i, hb, u, src, token_bank(ph, hb))
                    if t is not None:
                        turn_rest(t, u)

            def turn(t, tiles):
                for k in tiles:
                    if k % TB == 0:
                        if t:
                            pe.wait_ge(h_new, NH * (NB * (t - 1) + k // TB + 1))
                        else:
                            pe.wait_ge(x_loaded[0], 16)
                            pe.wait_ge(x_loaded[1], 16)
                    if k >= 4:
                        pe.wait_ge(x_ready, KT * t + k - 4 + 1)
                    for half in range(NH):
                        tr = pe.transpose(turned(k)[:, half * P:(half + 1) * P], h[:, half, k * P:(k + 1) * P],
                                          ident[:, :])
                    tr.then_inc(x_turned, 1)

            def turn_rest(t, u):
                if u == 0:
                    turn(t, range(4, 8))
                if u == 1:
                    turn(t, range(8, 12))
                if u == 3:
                    turn(t, range(12, KT))
                if u == 6:
                    pe.wait_ge(diag_ready, t + 1)
                    for half in range(NH):
                        mm = pe.matmul(ps[:, 4, half * P:(half + 1) * P], ones[:, :], diag[:, half, :],
                                       start=True, stop=True)
                    mm.then_inc(row_spread, 1)

            pe.wait_ge(constants, 7)
            pe.wait_ge(gains_loaded, 16 * 4)
            pe.transpose(ps[:, 3, 0:NGAIN], gain_rows[0:NGAIN, :], ident[0:NGAIN, 0:NGAIN]).then_inc(gains_turned, 1)
            turn(0, range(0, 4))
            pe.wait_ge(gains_ready, 1)
            tokens_out(gate_v, 0, x_parts, x_ready, lambda u: UK * u + UK, t=0)
            pe.wait_ge(spatial_masked, 1)
            pe.wait_ge(row_ready, 1)
            for g in range(G):
                tr = pe.transpose(ps[:, 4 + g // 4, (g % 4) * P:(g % 4 + 1) * P], ws_nat[:, g, :], ident[:, :])
            tr.then_inc(spatial_turned, 1)
            for hb in range(2):
                tokens_out_block(gate_v, 1, hb, x_parts, x_ready, lambda u: UK * u + UK)
                if hb == 0:
                    pe.wait_ge(ws_ready, 1)
                    pe.wait_ge(taps_loaded, 16 * 4)
                    for row in range(2 * (TAPS + 1)):
                        c = (row % (TAPS + 1)) * 2 * FT
                        tr = pe.transpose(ps[:, 4 + row // (TAPS + 1), c:c + 2 * FT], conv_rows[0:2 * FT, row, :],
                                          ident[0:2 * FT, 0:2 * FT])
                    tr.then_inc(taps_turned, 1)
            pe.wait_ge(taps_ready, 1)
            with pe.Fori(0, gate_u.pairs) as i:
                columns_out(gate_u, i, x_parts, x_ready, 0, flip=1)

            pe.wait_ge(v_normed, NH)
            pe.wait_ge(bias_loaded, 16)
            pe.wait_ge(evacuated, gate_u.block_end - 1)
            for g2 in range(G // 2):
                if g2 == 4:
                    pe.wait_ge(evacuated, gate_u.block_end)
                bank = mixing_bank(g2)
                for j in range(4):
                    pe.matmul(ps[:, bank, j * P:(j + 1) * P], ones[0:1, :], bias_row[0:1, 2 * g2 + j // 2, :],
                              start=(j == 0), stop=False, skip_group_check=True)
                for j in range(4):
                    g, chunk = 2 * g2 + j // 2, j % 2
                    mm = pe.matmul(ps[:, bank, j * P:(j + 1) * P], v_nat[:, chunk, g, :], ws_t[:, g, :],
                                   start=False, stop=(j == 3), skip_group_check=True)
                mm.then_inc(group_mixed, 1)
            pe.wait_ge(group_gated, 4)
            with pe.Fori(0, a_out.pairs) as i:
                tokens_out(a_out, i, mix_parts, group_ready, lambda u: u + 1)

            for layer in range(2):
                t = 1 + 2 * layer
                turn(t, range(0, 4))
                columns_out(UP[layer], 0, x_parts, x_ready, KT * t, t=t)
                with pe.Fori(1, FP) as i:
                    columns_out(UP[layer], i, x_parts, x_ready, KT * t)
                with pe.Fori(0, DOWN[layer].pairs) as i:
                    tokens_out(DOWN[layer], i, g_parts, g_ready, lambda u: layer * FP + (UK * u + 1) // TB + 1)
                if layer == 1:
                    break

                turn(2, range(0, 4))
                columns_out(q_in, 0, x_parts, x_ready, KT * 2, t=2)
                with pe.Fori(1, q_in.pairs) as i:
                    columns_out(q_in, i, x_parts, x_ready, KT * 2)
                with pe.Fori(0, k_in.pairs) as i:
                    columns_out(k_in, i, kv_parts, x_ready, KT * 2)

                def score(j):
                    pe.wait_ge(combined, NB + 2 * FP + 2 * NB)
                    if j:
                        pe.wait_ge(att_dve, 4 * (j - 1) + 3)
                    for a in range(2):
                        hd = 2 * j + a
                        pe.matmul(ps[:, 4 + a, 0:T], k_t[:, hd, 0:P], q_t[:, hd, :], start=True, stop=True)
                        mm = pe.matmul(ps[:, 4 + a, T:ATT], k_t[:, hd, P:T], q_t[:, hd, P:T], start=True, stop=True)
                    mm.then_inc(scored, 1)

                def sum_later(j):
                    pe.wait_ge(att_dve, 4 * j + 2)
                    if j:
                        pe.wait_ge(att_dve, 4 * (j - 1) + 4)
                    for a in range(2):
                        pe.matmul(ps[:, 6 + a, 0:ATT], later[:, :], att_sp[:, a, :], start=True, stop=False,
                                  skip_group_check=True)
                        mm = pe.matmul(ps[:, 6 + a, P:T], ones[:, :], att_sp[:, a, T:ATT], start=False, stop=True,
                                       skip_group_check=True)
                    mm.then_inc(summed, 1)

                def weight_values(j):
                    pe.wait_ge(evacuated, v_in.block0 + j // 2 + 1)
                    pe.wait_ge(att_ready, STEPS)
                    if j >= 4:
                        pe.wait_ge(o_ready, j - 3)
                    bank = weighted_bank(j)
                    for a in range(2):
                        hd = 2 * j + a
                        pe.matmul(ps[:, bank, a * T:(a + 1) * T], val[:, 0, hd * P:(hd + 1) * P], att[:, hd, 0:T],
                                  start=True, stop=False, skip_group_check=True)
                        mm = pe.matmul(ps[:, bank, a * T + P:(a + 1) * T], val[:, 1, hd * P:(hd + 1) * P],
                                       att[:, hd, T:ATT], start=False, stop=True, skip_group_check=True)
                    mm.then_inc(weighted, 1)

                for n in range(V_UNITS + b_out.units):
                    b, u = n // U, n % U
                    hb = b % 2
                    pe.wait_ge(unit_split, v_in.first + n + 1)
                    if b < NB:
                        if u == 0:
                            pe.wait_ge(evacuated, v_in.block0 + b - 1)
                        tokens_out_unit(v_in, 0, hb, u, kv_parts, token_bank(v_in, hb))
                    else:
                        pe.wait_ge(o_ready, u + 1)
                        if u == 0:
                            pe.wait_ge(evacuated, b_out.block0 - 1)
                        tokens_out_unit(b_out, 0, 0, u, o_parts, token_bank(b_out, 0))
                    j = step_at(n, SUMS)
                    if j is not None:
                        sum_later(j)
                    j = step_at(n, SCORES)
                    if j is not None:
                        score(j)
                    for j in range(STEPS):
                        if n == WEIGHTED[j]:
                            weight_values(j)
                tokens_out_block(b_out, 0, 1, o_parts, o_ready, lambda u: u + 1)
                with pe.Fori(1, b_out.pairs) as i:
                    tokens_out(b_out, i, o_parts, o_ready, lambda u: u + 1)


_INS = ['x', 'pre_mix_g', 'post_mix_g', 'pre_ffn_g', 'post_ffn_g', 'a_w_in', 'a_v_norm_g', 'a_w_spatial',
        'a_b_spatial', 'a_w_out', 'kv_norm_g', 'w_k', 'w_v', 'b_w_q', 'b_w_o', 'ffn_w_up', 'ffn_conv_w',
        'ffn_conv_b', 'ffn_w_down']


def kernel(**inputs):
    import numpy as np
    import concourse.bacc as bacc
    from concourse.bass_utils import run_bass_kernel_spmd

    nc = bacc.Bacc("TRN2", target_bir_lowering=False, num_devices=1)
    arrays, args = {}, []
    for name in _INS:
        a = np.ascontiguousarray(inputs[name])
        arrays[f"in_{name}"] = a
        args.append(nc.dram_tensor(f"in_{name}", a.shape, mybir.dt.from_np(a.dtype), kind="ExternalInput").ap())
    args.append(nc.dram_tensor("out", arrays["in_x"].shape, F32, kind="ExternalOutput").ap())
    build_trunk(nc, *args)
    r = run_bass_kernel_spmd(nc, [arrays], core_ids=[0])
    return r.results[0]["out"]
```

```python
from contextlib import ExitStack

import concourse.bass as bass
from concourse import mybir

ALU = mybir.AluOpType
ACT = mybir.ActivationFunctionType
AX = mybir.AxisListType
F32 = mybir.dt.float32
F32R = mybir.dt.float32r

P = 128
BLK = 512
UK = 2
RING = 4
EPS = 1e-6
HI, LO = 0, 1
SBUF_START = 16512


class Phase:

    def __init__(self, before, w, starts, step, pairs):
        self.w, self.starts, self.step, self.pairs = w, starts, step, pairs
        self.units = w.shape[0] // (UK * P)
        self.first = before.end if before else 0
        self.block0 = before.block_end if before else 0
        self.end = self.first + 2 * pairs * self.units
        self.block_end = self.block0 + 2 * pairs

    def column(self, i, h):
        return self.starts[h] + i * self.step

    def unit(self, b):
        return self.first + b * self.units


def build_trunk(nc, x, pre_mix_g, post_mix_g, pre_ffn_g, post_ffn_g, a_w_in, a_v_norm_g, a_w_spatial,
                a_b_spatial, a_w_out, kv_norm_g, w_k, w_v, b_w_q, b_w_o, ffn_w_up, ffn_conv_w,
                ffn_conv_b, ffn_w_down, out):
    _, T, D = x.shape
    NH = T // P
    KT = D // P
    G = a_w_spatial.shape[1]
    FF = ffn_w_down.shape[1]
    FT = FF // P
    HEADS = w_k.shape[1] // P
    NB = D // BLK
    TB = BLK // P
    FP = FF // BLK
    TAPS = ffn_conv_w.shape[1]
    PAD = TAPS - 1
    ATT = T + P
    STEPS = HEADS // 2
    LAST = NB - 1
    SCALE = float(P) ** -0.5
    assert T == 2 * P and G == KT and HEADS == KT and a_w_spatial.shape[2] == P

    gate_v = Phase(None, a_w_in[0], (D, D + BLK), 2 * BLK, NB // 2)
    gate_u = Phase(gate_v, a_w_in[0], (0, BLK), 2 * BLK, NB // 2)
    a_out = Phase(gate_u, a_w_out[0], (0, BLK), 2 * BLK, NB // 2)
    up0 = Phase(a_out, ffn_w_up[0], (0, FF), BLK, FP)
    down0 = Phase(up0, ffn_w_down[0], (0, BLK), 2 * BLK, NB // 2)
    q_in = Phase(down0, b_w_q[0], (0, BLK), 2 * BLK, NB // 2)
    k_in = Phase(q_in, w_k, (0, BLK), 2 * BLK, NB // 2)
    v_in = Phase(k_in, w_v, (0, BLK), 2 * BLK, NB // 2)
    b_out = Phase(v_in, b_w_o[0], (0, BLK), 2 * BLK, NB // 2)
    up1 = Phase(b_out, ffn_w_up[1], (0, FF), BLK, FP)
    down1 = Phase(up1, ffn_w_down[1], (0, BLK), 2 * BLK, NB // 2)
    phases = [gate_v, gate_u, a_out, up0, down0, q_in, k_in, v_in, b_out, up1, down1]
    UP, DOWN = (up0, up1), (down0, down1)
    NORMED = (a_out, down0, b_out, down1)
    POST_GAIN = (post_mix_g[0], post_ffn_g[0], post_mix_g[1], post_ffn_g[1])

    at = {"next": SBUF_START}

    def region(nbytes):
        start = at["next"]
        at["next"] += (nbytes + 31) // 32 * 32
        return start

    def place(name, shape, dtype, start):
        return nc.alloc_sbuf_tensor_at(name, [shape[0], *shape[1:]], dtype, offset=start)

    def sb(name, shape, dtype=F32):
        size = 4
        for n in shape[1:]:
            size *= n
        return place(name, shape, dtype, region(size))

    KB = 1024
    h = sb("h", [P, NH, D])
    raw = sb("raw", [P, RING, UK, BLK])
    w_hi = sb("w_hi", [P, RING, UK, BLK], F32R)
    w_lo = sb("w_lo", [P, RING, UK, BLK], F32R)

    x_at = region(32 * KB)
    x_parts = place("x_parts", [P, KT, 2, T], F32R, x_at)
    post_gain = place("post_gain", [P, D], F32, x_at)
    mixed = place("mixed", [P, NB, NH, BLK], F32, x_at + 16 * KB)
    att = place("att", [P, HEADS, ATT], F32, x_at)
    log_beta = place("log_beta", [P, 2, ATT], F32, x_at + 24 * KB)
    att_exp = place("att_exp", [P, 2, ATT], F32, x_at + 27 * KB)

    arena = region(FT * 2 * T * 4)
    u_t = place("u_t", [P, KT, T], F32, arena)
    v_nat = place("v_nat", [P, NH, G, P], F32, arena + 16 * KB)
    mix_parts = place("mix_parts", [P, KT, 2, T], F32R, arena + 32 * KB)
    ws_t = place("ws_t", [P, G, P], F32, arena + 64 * KB)
    v_gain = place("v_gain", [P, D], F32, arena + 72 * KB)
    bias_row = place("bias_row", [1, G, P], F32, arena + 72 * KB)
    bias_parts = place("bias_parts", [2, G, P], F32R, arena + 56 * KB)
    bias_low = place("bias_low", [1, G, P], F32R, arena + 48 * KB)
    v_square = place("v_square", [P, G, P], F32, arena + 80 * KB)
    ws_nat = place("ws_nat", [P, G, P], F32, arena + 32 * KB)
    gain_rows = place("gain_rows", [P, P], F32, arena + 40 * KB)
    conv_rows = place("conv_rows", [P, 2 * (TAPS + 1), P], F32, arena + 41 * KB)
    g_parts = place("g_parts", [P, FT, 2, T], F32R, arena)
    val = place("val", [P, NH, D], F32, arena)
    q_t = place("q_t", [P, HEADS, T], F32, arena + 16 * KB)
    k_t = place("k_t", [P, HEADS, T], F32, arena + 32 * KB)
    kv_parts = place("kv_parts", [P, KT, 2, T], F32R, arena + 48 * KB)
    kv_raw = place("kv_raw", [P, KT, 2, T], F32, arena + 48 * KB)
    o_parts = place("o_parts", [P, KT, 2, T], F32R, arena + 16 * KB)

    low_at = region(TB * T * 4)
    low = place("low", [P, TB, T], F32, low_at)
    sp_hi = place("sp_hi", [P, 2, ATT], F32R, low_at)
    conv_in = sb("conv_in", [P, TB, PAD + T])
    conv_at = region(TB * T * 4)
    conv = place("conv", [P, TB, T], F32, conv_at)
    v_sum = place("v_sum", [P, NH, G], F32, conv_at + KB)
    v_mean = place("v_mean", [P, NH, G], F32, conv_at + KB + 128)
    v_scale = place("v_scale", [P, NH, G], F32, conv_at + KB + 256)
    att_sp = place("att_sp", [P, 2, ATT], F32, conv_at)
    silu_at = region(TB * T * 4)
    silu = place("silu", [P, TB, T], F32, silu_at)
    sp_lo = place("sp_lo", [P, 2, ATT], F32R, conv_at)
    att_log = place("att_log", [P, 2, ATT], F32, silu_at)
    diag = place("diag", [P, NH, P], F32, conv_at)
    junk = place("junk", [P, NH, BLK], F32, silu_at)

    ident = sb("ident", [P, P])
    ones_r = sb("ones_r", [P, P], F32R)
    later = sb("later", [P, P], F32R)
    ones = sb("ones", [P, P])
    row_scale = sb("row_scale", [P, T])
    mask = sb("mask", [P, P])
    NGAIN = 5 * KT
    gains = sb("gains", [P, NGAIN])
    conv_cols = sb("conv_cols", [P, 2, TAPS + 1, 2 * FT])
    half_neg = sb("half_neg", [P, KT * NH])
    block_sq = sb("block_sq", [P, NH, NB])
    post_sum = sb("post_sum", [P, NH])
    post_base = sb("post_base", [P, NH])
    post_mean = sb("post_mean", [P, NH])
    post_scale = sb("post_scale", [P, NH])
    stream_sq = sb("stream_sq", [P, NH, NB])
    pre_sum = sb("pre_sum", [P, NH])
    pre_mean = sb("pre_mean", [P, NH])
    pre_scale = sb("pre_scale", [P, NH])
    assert at["next"] <= nc.sbuf_usable_end, at["next"] - nc.sbuf_usable_end

    PRE_GAIN = (0, 2 * KT, KT, 3 * KT)
    KV_GAIN = 4 * KT
    KV_NORM = 2

    with ExitStack() as ctx:
        ps = ctx.enter_context(nc.psum_tensor("ps", [P, 8, BLK], F32))

        def sem(name):
            return ctx.enter_context(nc.semaphore(name))

        x_loaded = [sem(f"x_loaded{c}") for c in range(NB)]
        mix_gains_loaded = sem("mix_gains_loaded")
        gains_loaded = sem("gains_loaded")
        taps_loaded = sem("taps_loaded")
        spatial_loaded = sem("spatial_loaded")
        v_gain_loaded = sem("v_gain_loaded")
        bias_loaded = sem("bias_loaded")
        bias_hi = sem("bias_hi")
        bias_split = sem("bias_split")
        bias_ready = sem("bias_ready")
        post_gain_loaded = sem("post_gain_loaded")
        constants = sem("constants")
        spatial_masked = sem("spatial_masked")
        gains_turned = sem("gains_turned")
        taps_turned = sem("taps_turned")
        spatial_turned = sem("spatial_turned")
        gains_ready = sem("gains_ready")
        taps_ready = sem("taps_ready")
        ws_ready = sem("ws_ready")
        raw_loaded = [sem(f"raw_loaded{i}") for i in range(RING)]
        unit_hi = sem("unit_hi")
        unit_split = sem("unit_split")
        unit_used = sem("unit_used")
        evacuated = sem("evacuated")
        low_copied = sem("low_copied")
        u_ready = sem("u_ready")
        v_step = sem("v_step")
        v_normed = sem("v_normed")
        group_mixed = sem("group_mixed")
        group_gated = sem("group_gated")
        group_hi = sem("group_hi")
        group_ready = sem("group_ready")
        half_done = sem("half_done")
        squared = sem("squared")
        post_meaned = sem("post_meaned")
        post_scaled = sem("post_scaled")
        h_new = [sem(f"h_new{half}") for half in range(NH)]
        pre_squared = sem("pre_squared")
        pre_meaned = sem("pre_meaned")
        pre_scaled = sem("pre_scaled")
        diag_ready = sem("diag_ready")
        row_spread = sem("row_spread")
        row_ready = sem("row_ready")
        combined = sem("combined")
        x_turned = sem("x_turned")
        x_hi_ready = sem("x_hi_ready")
        x_ready = sem("x_ready")
        kv_kept = sem("kv_kept")
        kv_hi_ready = sem("kv_hi_ready")
        kv_ready = sem("kv_ready")
        conv_step = sem("conv_step")
        silu_ready = sem("silu_ready")
        gated = sem("gated")
        g_hi_ready = sem("g_hi_ready")
        g_ready = sem("g_ready")
        scored = sem("scored")
        att_act = sem("att_act")
        att_dve = sem("att_dve")
        exponent_ready = sem("exponent_ready")
        weights_ready = sem("weights_ready")
        att_ready = sem("att_ready")
        summed = sem("summed")
        weighted = sem("weighted")
        o_hi_ready = sem("o_hi_ready")
        o_ready = sem("o_ready")
        dve_order = sem("dve_order")
        stored = sem("stored")

        def token_bank(ph, h_):
            return 2 * h_ + (4 if ph is a_out else 0)

        def mixing_bank(g2):
            return (g2 + 4) % 8

        def column_bank(h_, flip=0):
            return 4 * ((h_ + flip) % 2)

        def turned(k):
            return ps[:, 4 + k % 4, 0:T]

        SCORES, SUMS, SOFTPLUS, SPLIT, WEIGHTS = 2, 5, 6, 7, 9

        STREAM_BEFORE = [0, 2, 3, 4]

        V_UNITS = NB * v_in.units
        WEIGHTED = [28, 28, 29, 29, 31, 31, 34, 34]
        OUT_SLOT = [32, 32, 33, 33, 35, 35, 38, 38]

        def weighted_bank(j):
            return 4 + j % 4

        def kv_tiles(b):
            return range(KT * (b - 1) // (NB - 1), KT * b // (NB - 1))

        def step_at(n, offset):
            j = (n - offset) // 3
            return j if (n - offset) % 3 == 0 and 0 <= j < STEPS else None

        block = ctx.enter_context(nc.Block())

        @block.sync
        def _(sp):
            def load_stream(c):
                sp.dma_start(h[:, :, c * BLK:(c + 1) * BLK], x[0, :, c * BLK:(c + 1) * BLK].rearrange(
                    "(a p) d -> p a d", p=P)).then_inc(x_loaded[c], 16)

            def load_pair(ph, i, fresh=False):
                for hb in range(2):
                    for u in range(ph.units):
                        k = hb * ph.units + u
                        if fresh and k in STREAM_BEFORE:
                            load_stream(STREAM_BEFORE.index(k))
                        if not (fresh and k < RING):
                            sp.wait_ge(unit_split, i * (2 * ph.units) + (ph.first + k - RING + 1))
                        rows = ph.w[u * UK * P:(u + 1) * UK * P, bass.ds(ph.column(i, hb), BLK)]
                        sp.dma_start(raw[:, k % RING, :, :],
                                     rows.rearrange("(k p) n -> p k n", p=P)).then_inc(raw_loaded[k % RING], 16)

            for ph in phases:
                if ph is gate_v:
                    load_pair(ph, 0, fresh=True)
                with sp.Fori(1 if ph is gate_v else 0, ph.pairs) as i:
                    load_pair(ph, i)
            for half in range(NH):
                for c in range(NB):
                    sp.wait_ge(h_new[half], NB * (len(NORMED) - 1) + c + 1)
                    sp.dma_start(out[0, half * P:(half + 1) * P, c * BLK:(c + 1) * BLK],
                                 h[:, half, c * BLK:(c + 1) * BLK]).then_inc(stored, 16)
            sp.wait_ge(stored, 16 * NH * NB)

        @block.gpsimd
        def _(pool):
            pool.memset(half_neg[:, :], -0.5).then_inc(constants, 1)
            pool.memset(ident[:, :], 0.0).then_inc(constants, 1)
            pool.memset(ones[:, :], 1.0).then_inc(constants, 1)
            pool.memset(mask[:, :], 1.0).then_inc(constants, 1)
            pool.wait_ge(constants, 4)
            pool.affine_select(out=ident[:, :], in_=ident[:, :], compare_op=ALU.not_equal, fill=1.0,
                               base=0, pattern=[[-1, P]], channel_multiplier=1).then_inc(constants, 1)
            pool.affine_select(out=later[:, :], in_=ones[:, :], compare_op=ALU.is_gt, fill=0.0,
                               base=0, pattern=[[-1, P]], channel_multiplier=1).then_inc(constants, 1)
            pool.tensor_copy(ones_r[:, :], ones[:, :]).then_inc(constants, 1)
            pool.affine_select(out=mask[:, :], in_=mask[:, :], compare_op=ALU.is_gt, fill=0.0,
                               base=0, pattern=[[1, P]], channel_multiplier=-1).then_inc(constants, 1)

            def rsqrt(to, of, n, ready, done, count):
                pool.wait_ge(ready, count)
                pool.tensor_tensor(to, of, half_neg[:, 0:n], ALU.pow).then_inc(done, 1)

            def pre_rsqrt(t):
                rsqrt(pre_scale[:, :], pre_mean[:, :], NH, pre_meaned, pre_scaled, t + 1)

            def load_post_gain(s):
                pool.dma_start(post_gain[:, :], POST_GAIN[s].unsqueeze(0).to_broadcast([P, D])
                               ).then_inc(post_gain_loaded, 16)

            pool.wait_ge(x_loaded[NB - 1], 16)
            pool.dma_start(ws_nat[:, :, :], a_w_spatial[0].rearrange("g t s -> t g s")).then_inc(spatial_loaded, 16)
            for layer in range(2):
                row = layer * (TAPS + 1)
                pool.dma_start(conv_rows[0:2 * FT, row:row + TAPS, :], ffn_conv_w[layer].rearrange("t (f p) -> f t p", p=P)
                               ).then_inc(taps_loaded, 16)
                pool.dma_start(conv_rows[0:2 * FT, row + TAPS, :], ffn_conv_b[layer].rearrange("(f p) -> f p", p=P)
                               ).then_inc(taps_loaded, 16)
            pool.dma_start(v_gain[:, :], a_v_norm_g[0:1, :].to_broadcast([P, D])).then_inc(v_gain_loaded, 16)
            pre_rsqrt(0)
            pool.wait_ge(spatial_loaded, 16)
            pool.affine_select(out=ws_nat[:, :, :], in_=ws_nat[:, :, :], compare_op=ALU.is_ge, fill=0.0,
                               base=0, pattern=[[0, G], [-1, P]], channel_multiplier=1).then_inc(spatial_masked, 1)
            rsqrt(v_scale[:, :, :].rearrange("p a g -> p (a g)"), v_mean[:, :, :].rearrange("p a g -> p (a g)"),
                  NH * G, v_step, v_step, 5)
            for half in range(NH):
                pool.wait_ge(v_step, 7 + half)
                if half == 0:
                    pool.wait_ge(v_gain_loaded, 16)
                vh = v_nat[:, half, :, :].rearrange("p g d -> p (g d)")
                pool.tensor_tensor(vh, vh, v_gain[:, :], ALU.mult).then_inc(v_normed, 1)
            pool.wait_ge(v_normed, NH)
            pool.dma_start(bias_row[:, :, :], a_b_spatial).then_inc(bias_loaded, 16)
            pool.wait_ge(bias_split, 1)
            pool.dma_start(bias_parts[1:2, :, :], bias_low[:, :, :]).then_inc(bias_ready, 16)
            for s, ph in enumerate(NORMED):
                if s == 2:
                    for j in range(STEPS):
                        pool.wait_ge(weights_ready, j + 1)
                        for c in (0, T):
                            heads = att[:, 2 * j:2 * j + 2, c:c + P]
                            last = pool.affine_select(out=heads, in_=heads, compare_op=ALU.is_gt, fill=0.0, base=0,
                                                      pattern=[[0, 2], [1, P]], channel_multiplier=-1)
                        last.then_inc(att_ready, 1)
                    pool.wait_ge(weighted, STEPS)
                else:
                    pool.wait_ge(unit_used, ph.first)
                load_post_gain(s)
                for half in range(NH):
                    rsqrt(post_scale[:, half:half + 1], post_mean[:, half:half + 1], 1,
                          post_meaned, post_scaled, NH * s + half + 1)
                if s + 1 < len(NORMED):
                    pre_rsqrt(s + 1)

        @block.scalar
        def _(act):
            def units(base, a, b):
                for k in range(a, b):
                    slot = k % RING
                    if isinstance(base, int):
                        act.wait_ge(raw_loaded[slot], 16 * ((base + k) // RING + 1))
                    else:
                        act.wait_ge(raw_loaded[slot], base_loads[0] + 16 * (k // RING + 1))
                    if not isinstance(base, int) or base + k >= RING:
                        act.wait_ge(unit_used, base + (k - RING + 1))
                    act.copy(w_hi[:, slot, :, :], raw[:, slot, :, :]).then_inc(unit_hi, 1)

            base_loads = [None]

            def copy_low(block_no, used, bank, scale=None):
                act.wait_ge(unit_used, used)
                act.wait_ge(evacuated, block_no)
                src = ps[:, bank:bank + TB, T:2 * T]
                ins = act.copy(low[:, :, :], src) if scale is None else act.mul(low[:, :, :], src, scale)
                ins.then_inc(low_copied, 1)

            def square(s, b, halves=range(NH)):
                ph = NORMED[s]
                bank = token_bank(ph, b % 2)
                for half in halves:
                    if s + b and half == 0:
                        act.wait_ge(squared, NH * (NB * s + b))
                    if half == 0:
                        act.wait_ge(half_done, NB * s + b + 1)
                    else:
                        act.wait_ge(unit_used, ph.unit(b + 1))
                    act.activation(junk[:, half, :], ps[:, bank + half, :], ACT.Square,
                                   accum_out=block_sq[:, half, b:b + 1]).then_inc(squared, 1)

            def square_stream(t, c):
                if t:
                    for half in range(NH):
                        act.wait_ge(h_new[half], NB * (t - 1) + c + 1)
                    act.wait_ge(squared, NH * NB * t)
                else:
                    act.wait_ge(x_loaded[c], 16)
                if t + c:
                    act.wait_ge(pre_squared, NB * t + c)
                for half in range(NH):
                    last = act.activation(junk[:, half, :], h[:, half, c * BLK:(c + 1) * BLK], ACT.Square,
                                          accum_out=stream_sq[:, half, c:c + 1])
                last.then_inc(pre_squared, 1)

            def x_high(t, tiles):
                for k in tiles:
                    act.wait_ge(x_turned, KT * t + k + 1)
                    c = PRE_GAIN[t] + k
                    act.activation(x_parts[:, k, HI, :], turned(k), ACT.Copy, scale=gains[:, c:c + 1]
                                   ).then_inc(x_hi_ready, 1)
                if t == KV_NORM:
                    for k in tiles:
                        act.wait_ge(x_ready, KT * t + k + 1)
                        act.copy(kv_raw[:, k, LO, :], turned(k)).then_inc(kv_kept, 1)

            def kv_high(tiles):
                for k in tiles:
                    act.wait_ge(kv_kept, k + 1)
                    act.activation(kv_parts[:, k, HI, :], kv_raw[:, k, LO, :], ACT.Copy,
                                   scale=gains[:, KV_GAIN + k:KV_GAIN + k + 1]).then_inc(kv_hi_ready, 1)

            act.dma_start(gain_rows[0:2 * KT, :], pre_mix_g.rearrange("l (k p) -> (l k) p", p=P)
                          ).then_inc(mix_gains_loaded, 16)
            act.preload_act_table_set("gelu_apprx_tanh_and_others")
            act.dma_start(gain_rows[2 * KT:4 * KT, :], pre_ffn_g.rearrange("l (k p) -> (l k) p", p=P)
                          ).then_inc(gains_loaded, 16)
            act.dma_start(gain_rows[4 * KT:5 * KT, :], kv_norm_g.rearrange("(k p) -> k p", p=P)).then_inc(gains_loaded, 16)
            def turn_and_split(t, ph):
                units(ph.first, RING - 1, RING)
                for c in (0, 1, 2):
                    x_high(t, range(c * TB, (c + 1) * TB))
                    square_stream(t, c)
                units(ph.first, RING, RING + 1)
                square_stream(t, NB - 1)
                units(ph.first, RING + 1, RING + 2)
                x_high(t, range((NB - 1) * TB, KT))
                units(ph.first, RING + 2, ph.units)

            act.wait_ge(gains_ready, 1)
            x_high(0, range(0, 2))
            units(0, 0, 1)
            x_high(0, range(2, TB))
            units(0, 1, 2)
            square_stream(0, 0)
            x_high(0, range(TB, 2 * TB))
            units(0, 2, 3)
            square_stream(0, 1)
            x_high(0, range(2 * TB, 3 * TB))
            units(0, 3, RING + 2)
            x_high(0, range(3 * TB, KT))
            square_stream(0, 2)
            square_stream(0, 3)
            units(0, RING + 2, gate_v.units)

            def gelu_v(b):
                act.wait_ge(unit_used, gate_v.unit(b + 1))
                act.wait_ge(pre_scaled, 1)
                bank = token_bank(gate_v, b % 2)
                for half in range(NH):
                    last = act.activation(v_nat[:, half, b * TB:(b + 1) * TB, :].rearrange("p g d -> p (g d)"),
                                          ps[:, bank + half, :], ACT.Gelu_apprx_tanh,
                                          scale=pre_scale[:, half:half + 1])
                last.then_inc(evacuated, 1)

            def gelu_u(b):
                act.wait_ge(combined, b + 1)
                tiles = u_t[:, b * TB:(b + 1) * TB, :]
                act.activation(tiles, tiles, ACT.Gelu_apprx_tanh).then_inc(u_ready, 1)

            U = gate_v.units
            for b in range(1, NB):
                units(gate_v.unit(b), 0, RING)
                gelu_v(b - 1)
                if b == 2:
                    act.wait_ge(spatial_turned, 1)
                    act.copy(ws_t[:, :, :].rearrange("p (b g) s -> p b (g s)", b=4), ps[:, 4:8, :]
                             ).then_inc(ws_ready, 1)
                units(gate_v.unit(b), RING, U)
            for b in range(NB):
                units(gate_u.unit(b), 0, RING)
                if b == 0:
                    gelu_v(LAST)
                    units(gate_u.unit(b), RING, U)
                else:
                    copy_low(gate_u.block0 + b - 1, gate_u.unit(b), column_bank(b - 1, 1))
                    units(gate_u.unit(b), RING, RING + 2)
                    gelu_u(b - 1)
                    units(gate_u.unit(b), RING + 2, U)
                if b == 2:
                    act.wait_ge(bias_loaded, 16)
                    act.copy(bias_parts[0:1, :, :], bias_row[:, :, :]).then_inc(bias_hi, 1)

            def group_high(g2):
                act.wait_ge(group_gated, g2 + 1)
                if g2 == 6:
                    act.wait_ge(group_mixed, G // 2)
                act.copy(mix_parts[:, 2 * g2:2 * g2 + 2, HI, :], v_square[:, :, :].rearrange(
                    "p g d -> p (g d)")[:, (g2 % 4) * 2 * T:(g2 % 4 + 1) * 2 * T].rearrange("p (g t) -> p g t", g=2)
                         ).then_inc(group_hi, 1)

            units(a_out.first, 0, RING - 1)
            copy_low(gate_u.block_end - 1, gate_u.end, column_bank(LAST % 2, 1))
            for g2 in range(2):
                group_high(g2)
            units(a_out.first, RING - 1, RING)
            gelu_u(LAST)
            for g2 in range(2, 4):
                group_high(g2)
            for g2 in range(4, 8):
                units(a_out.first, g2, g2 + 1)
                group_high(g2)
            for b in range(1, NB):
                units(a_out.unit(b), 0, RING)
                square(0, b - 1)
                units(a_out.unit(b), RING, U)

            act.wait_ge(taps_ready, 1)

            def after_normed(s, nxt):
                square(s, LAST, (0,))
                units(nxt.first, 0, RING - 1)
                square(s, LAST, (1,))
                turn_and_split(s + 1, nxt)

            def ffn_gate_silu(ff_block, j):
                act.wait_ge(conv_step, 3 * ff_block + 3)
                if not isinstance(j, int) or j:
                    act.wait_ge(gated, j)
                act.activation(silu[:, :, :], conv[:, :, :], ACT.Silu).then_inc(silu_ready, 1)

            def ffn_high(layer, i):
                act.wait_ge(gated, i + layer * FP + 1)
                act.copy(g_parts[:, bass.ds(i * TB, TB), HI, :], conv[:, :, :]).then_inc(g_hi_ready, 1)

            def ffn_up(layer, s):
                ph = UP[layer]
                low0 = 4 + 8 * layer + 2 * FP * layer

                def gate_part(i):
                    base = i * (2 * U) + ph.first
                    units(base, U, U + RING)
                    copy_low(i * 2 + ph.block0, base + U, column_bank(0))
                    units(base, U + RING, 2 * U)
                    ffn_gate_silu(i * 2 + 2 * FP * layer, i + FP * layer)

                after_normed(s, ph)
                gate_part(0)
                with act.Fori(1, ph.pairs) as i:
                    base = i * (2 * U) + ph.first
                    base_loads[0] = i * (16 * 2 * U // RING) + 16 * ph.first // RING
                    units(base, 0, RING)
                    copy_low(i * 2 + (ph.block0 - 1), base, column_bank(1))
                    units(base, RING, U - 1)
                    ffn_high(layer, i - 1)
                    units(base, U - 1, U)
                    gate_part(i)

            def ffn_down(layer, s):
                ph, up = DOWN[layer], UP[layer]
                units(ph.first, 0, RING)
                copy_low(up.block_end - 1, up.end, column_bank(1))
                units(ph.first, RING, U - 1)
                ffn_high(layer, FP - 1)
                units(ph.first, U - 1, ph.units)
                for b in range(1, NB):
                    units_of(ph, b, 0, RING)
                    square(s, b - 1)
                    units_of(ph, b, RING, ph.units)

            def units_of(ph, b, a, e):
                units(ph.first, b * ph.units + a, b * ph.units + e)

            ffn_up(0, 0)
            ffn_down(0, 1)

            after_normed(1, q_in)
            for ph in (q_in, k_in):
                for b in range(NB):
                    if ph is q_in and b == 0:
                        continue
                    units(ph.unit(b), 0, RING)
                    done, bank = ph.block0 + b - 1, column_bank((b + 1) % 2)
                    scaled = (ph is q_in) or b == 0
                    copy_low(done, ph.unit(b), bank, SCALE if scaled else None)
                    units(ph.unit(b), RING, RING + 2)
                    if ph is q_in:
                        kv_high(kv_tiles(b))
                    units(ph.unit(b), RING + 2, U)

            def copy_value(b):
                act.wait_ge(unit_used, v_in.unit(b + 1))
                bank = token_bank(v_in, b % 2)
                for half in range(NH):
                    last = act.activation(val[:, half, b * BLK:(b + 1) * BLK], ps[:, bank + half, :], ACT.Copy,
                                          scale=pre_scale[:, half:half + 1])
                last.then_inc(evacuated, 1)

            def att_softplus_log(j):
                act.wait_ge(scored, j + 1)
                if j:
                    act.wait_ge(att_dve, 4 * (j - 1) + 3)
                act.activation(att_log[:, :, :], ps[:, 4:6, 0:ATT], ACT.Abs).then_inc(att_act, 1)
                act.wait_ge(att_act, 4 * j + 1)
                act.activation(att_log[:, :, :], att_log[:, :, :], ACT.Exp, scale=-1.0).then_inc(att_act, 1)
                act.wait_ge(att_act, 4 * j + 2)
                act.activation(att_log[:, :, :], att_log[:, :, :], ACT.Ln, bias=1.0).then_inc(att_act, 1)

            def att_split(j):
                act.wait_ge(att_dve, 4 * j + 2)
                if j:
                    act.wait_ge(summed, j)
                act.copy(sp_hi[:, :, :], att_sp[:, :, :]).then_inc(att_act, 1)

            def att_weight(j):
                act.wait_ge(exponent_ready, j + 1)
                act.activation(att[:, 2 * j:2 * j + 2, :], att_exp[:, :, :], ACT.Exp).then_inc(weights_ready, 1)

            def out_high(j):
                act.wait_ge(weighted, j + 1)
                act.copy(o_parts[:, 2 * j:2 * j + 2, HI, :], ps[:, weighted_bank(j), :].rearrange("p (a t) -> p a t", a=2)
                         ).then_inc(o_hi_ready, 1)

            act.preload_act_table_set("natural_log_exp_and_others")
            for n in range(V_UNITS + b_out.units):
                units(v_in.first, n, n + 1)
                if n == RING - 1:
                    copy_low(k_in.block_end - 1, k_in.end, column_bank(1))
                if (n - RING + 1) % U == 0 and 0 < (n - RING + 1) // U <= NB:
                    copy_value((n - RING + 1) // U - 1)
                j = step_at(n, SOFTPLUS)
                if j is not None:
                    att_softplus_log(j)
                j = step_at(n, WEIGHTS)
                if j is not None:
                    att_weight(j)
                j = step_at(n, SPLIT)
                if j is not None:
                    att_split(j)
                for j in range(STEPS):
                    if n == OUT_SLOT[j]:
                        out_high(j)
            for b in range(1, NB):
                units(b_out.unit(b), 0, RING)
                square(2, b - 1)
                units(b_out.unit(b), RING, U)

            ffn_up(1, 2)
            ffn_down(1, 3)
            square(3, LAST)

        @block.vector
        def _(dve):
            def units(base, a, b):
                for k in range(a, b):
                    slot = k % RING
                    dve.wait_ge(unit_hi, base + (k + 1))
                    dve.tensor_tensor(w_lo[:, slot, :, :], raw[:, slot, :, :], w_hi[:, slot, :, :].bitcast(F32),
                                      ALU.subtract).then_inc(unit_split, 1)

            ordered = [0]

            def link(ins):
                ordered[0] += 1
                ins.then_inc(dve_order, 1)
                dve.wait_ge(dve_order, ordered[0])

            def add_low(to, low_no, bank, scale=None):
                dve.wait_ge(low_copied, low_no)
                src = ps[:, bank:bank + TB, 0:T]
                if scale is None:
                    dve.tensor_tensor(to, src, low[:, :, :], ALU.add).then_inc(evacuated, 1)
                else:
                    dve.scalar_tensor_tensor(out=to, in0=src, scalar=scale, in1=low[:, :, :],
                                             op0=ALU.mult, op1=ALU.add).then_inc(evacuated, 1)

            def scale_tokens(to, block_no, low_no):
                dve.wait_ge(evacuated, block_no + 1)
                dve.tensor_tensor(to, to, row_scale[:, :].unsqueeze(1).to_broadcast([P, TB, T]), ALU.mult
                                  ).then_inc(combined, 1)

            def gain_block(s, b, halves=range(NH)):
                dve.wait_ge(post_gain_loaded, 16 * (s + 1))
                bank = token_bank(NORMED[s], b % 2)
                for half in halves:
                    dve.wait_ge(squared, NH * (NB * s + b) + half + 1)
                    last = dve.tensor_tensor(mixed[:, b, half, :], ps[:, bank + half, :],
                                             post_gain[:, b * BLK:(b + 1) * BLK], ALU.mult)
                    if half == NH - 1:
                        last.then_inc(evacuated, 1)
                return last

            def begin_post_norm(s):
                dve.wait_ge(squared, NH * (NB * s + LAST))
                link(dve.tensor_reduce(post_sum[:, :], block_sq[:, :, 0:LAST], AX.X, ALU.add))
                link(dve.tensor_scalar(post_base[:, :], post_sum[:, :], 1.0 / D, EPS, ALU.mult, ALU.add))

            def post_norm(s, half):
                dve.wait_ge(squared, NH * (NB * s + LAST) + half + 1)
                dve.tensor_scalar(post_mean[:, half:half + 1], block_sq[:, half, LAST:NB], 1.0 / D,
                                  post_base[:, half:half + 1], ALU.mult, ALU.add).then_inc(post_meaned, 1)
                last = gain_block(s, LAST, (half,))
                if half == 0:
                    link(last)

            def update_stream(s, c, half):
                dve.wait_ge(post_scaled, NH * s + half + 1)
                if half or c < LAST:
                    dve.wait_ge(evacuated, NORMED[s].block_end - 1 + c // LAST)
                hc = h[:, half, c * BLK:(c + 1) * BLK]
                dve.scalar_tensor_tensor(out=hc, in0=mixed[:, c, half, :],
                                         scalar=post_scale[:, half:half + 1], in1=hc,
                                         op0=ALU.mult, op1=ALU.add).then_inc(h_new[half], 1)

            def pre_means(t):
                dve.wait_ge(pre_squared, NB * (t + 1))
                link(dve.tensor_reduce(pre_sum[:, :], stream_sq[:, :, :], AX.X, ALU.add))
                dve.tensor_scalar(pre_mean[:, :], pre_sum[:, :], 1.0 / D, EPS, ALU.mult, ALU.add
                                  ).then_inc(pre_meaned, 1)

            def pre_diagonals(t):
                dve.wait_ge(pre_scaled, t + 1)
                for half in range(NH):
                    last = dve.tensor_scalar(diag[:, half, :], ident[:, :], pre_scale[:, half:half + 1], None, ALU.mult)
                last.then_inc(diag_ready, 1)

            def turn_and_split(t, ph):
                update_stream(t - 1, 0, 1)
                units(ph.first, 1, 2)
                x_low(t, range(0, TB))
                update_stream(t - 1, 1, 1)
                units(ph.first, 2, RING - 1)
                x_low(t, range(TB, 2 * TB))
                update_stream(t - 1, 2, 1)
                units(ph.first, RING - 1, RING)
                update_stream(t - 1, 3, 1)
                x_low(t, range(2 * TB, 3 * TB))
                units(ph.first, RING, RING + 2)
                pre_means(t)
                x_low(t, range(3 * TB, KT))
                pre_diagonals(t)
                units(ph.first, RING + 2, ph.units)

            def copy_row_scale(t):
                dve.wait_ge(row_spread, t + 1)
                dve.tensor_copy(row_scale[:, :], ps[:, 4, 0:T]).then_inc(row_ready, 1)

            def x_low(t, tiles):
                for k in tiles:
                    dve.wait_ge(x_hi_ready, KT * t + k + 1)
                    c = PRE_GAIN[t] + k
                    dve.scalar_tensor_tensor(out=x_parts[:, k, LO, :], in0=turned(k), scalar=gains[:, c:c + 1],
                                             in1=x_parts[:, k, HI, :].bitcast(F32),
                                             op0=ALU.mult, op1=ALU.subtract).then_inc(x_ready, 1)

            def kv_low(tiles):
                for k in tiles:
                    dve.wait_ge(kv_hi_ready, k + 1)
                    dve.scalar_tensor_tensor(out=kv_parts[:, k, LO, :], in0=kv_raw[:, k, LO, :],
                                             scalar=gains[:, KV_GAIN + k:KV_GAIN + k + 1],
                                             in1=kv_parts[:, k, HI, :].bitcast(F32),
                                             op0=ALU.mult, op1=ALU.subtract).then_inc(kv_ready, 1)

            link(dve.memset(conv_in[:, :, 0:PAD], 0.0))
            dve.wait_ge(gains_turned, 1)
            dve.tensor_copy(gains[:, 0:2 * KT], ps[:, 3, 0:2 * KT]).then_inc(gains_ready, 1)
            dve.wait_ge(gains_ready, 1)
            x_low(0, range(0, 2))
            units(0, 0, 1)
            x_low(0, range(2, TB))
            units(0, 1, 2)
            x_low(0, range(TB, 2 * TB))
            units(0, 2, 3)
            x_low(0, range(2 * TB, 3 * TB))
            units(0, 3, RING + 1)
            x_low(0, range(3 * TB, KT))
            units(0, RING + 1, RING + 3)
            pre_means(0)
            pre_diagonals(0)
            units(0, RING + 3, gate_v.units)
            U = gate_v.units
            units(gate_v.unit(1), 0, 3)
            copy_row_scale(0)
            units(gate_v.unit(1), 3, U)
            units(gate_v.unit(2), 0, U)
            units(gate_v.unit(3), 0, RING)
            dve.wait_ge(taps_turned, 1)
            dve.tensor_copy(gains[:, 2 * KT:NGAIN], ps[:, 6, 2 * KT:NGAIN])
            dve.tensor_copy(conv_cols[:, :, :, :].rearrange("p l t f -> p l (t f)"),
                            ps[:, 4:6, 0:(TAPS + 1) * 2 * FT]).then_inc(taps_ready, 1)
            units(gate_v.unit(3), RING, U)

            def square_v(half):
                if half == 0:
                    dve.wait_ge(evacuated, gate_v.block_end)
                dve.tensor_tensor(v_square[:, :, :], v_nat[:, half, :, :], v_nat[:, half, :, :], ALU.mult
                                  ).then_inc(v_step, 1)

            def sum_v(half):
                dve.wait_ge(v_step, 2 * half + 1)
                dve.tensor_reduce(v_sum[:, half, :], v_square[:, :, :], AX.X, ALU.add).then_inc(v_step, 1)

            def mean_v():
                dve.wait_ge(v_step, 4)
                dve.tensor_scalar(v_mean[:, :, :], v_sum[:, :, :], 1.0 / P, EPS, ALU.mult, ALU.add
                                  ).then_inc(v_step, 1)

            def norm_v(half):
                dve.wait_ge(v_step, 6)
                dve.tensor_tensor(v_nat[:, half, :, :], v_nat[:, half, :, :],
                                  v_scale[:, half, :].unsqueeze(2).to_broadcast([P, G, P]), ALU.mult
                                  ).then_inc(v_step, 1)

            def u_block(b):
                return u_t[:, b * TB:(b + 1) * TB, :]

            def add_u(b):
                add_low(u_block(b), b + 1, column_bank(b % 2, 1))
                scale_tokens(u_block(b), gate_u.block0 + b, b + 1)

            units(gate_u.unit(0), 0, RING)
            square_v(0)
            units(gate_u.unit(0), RING, RING + 1)
            sum_v(0)
            units(gate_u.unit(0), RING + 1, RING + 2)
            dve.wait_ge(v_step, 2)
            square_v(1)
            units(gate_u.unit(0), RING + 2, RING + 3)
            sum_v(1)
            units(gate_u.unit(0), RING + 3, U)
            mean_v()
            units(gate_u.unit(1), 0, RING)
            add_u(0)
            units(gate_u.unit(1), RING, RING + 1)
            norm_v(0)
            units(gate_u.unit(1), RING + 1, RING + 3)
            norm_v(1)
            units(gate_u.unit(1), RING + 3, U)
            for b in range(2, NB):
                units(gate_u.unit(b), 0, RING)
                add_u(b - 1)
                units(gate_u.unit(b), RING, U)
                if b == 2:
                    dve.wait_ge(bias_hi, 1)
                    dve.tensor_tensor(bias_low[:, :, :], bias_row[:, :, :], bias_parts[0:1, :, :].bitcast(F32),
                                      ALU.subtract).then_inc(bias_split, 1)

            def gate_place(g2):
                return v_square[:, :, :].rearrange("p g d -> p (g d)")[:, (g2 % 4) * 2 * T:(g2 % 4 + 1) * 2 * T]

            def gate_group(g2):
                dve.wait_ge(group_mixed, g2 + 1)
                dve.wait_ge(u_ready, g2 // 2 + 1)
                dve.tensor_tensor(gate_place(g2), ps[:, mixing_bank(g2), :],
                                  u_t[:, 2 * g2:2 * g2 + 2, :].rearrange("p g t -> p (g t)"), ALU.mult
                                  ).then_inc(group_gated, 1)

            def group_low(g2):
                dve.wait_ge(group_hi, g2 + 1)
                dve.tensor_tensor(mix_parts[:, 2 * g2:2 * g2 + 2, LO, :],
                                  gate_place(g2).rearrange("p (g t) -> p g t", g=2),
                                  mix_parts[:, 2 * g2:2 * g2 + 2, HI, :].bitcast(F32), ALU.subtract
                                  ).then_inc(group_ready, 1)

            units(a_out.first, 0, RING - 1)
            gate_group(0)
            gate_group(1)
            add_low(u_block(LAST), LAST + 1, column_bank(LAST % 2, 1))
            group_low(0)
            scale_tokens(u_block(LAST), gate_u.block0 + LAST, LAST + 1)
            group_low(1)
            units(a_out.first, RING - 1, RING)
            gate_group(2)
            gate_group(3)
            group_low(2)
            group_low(3)
            for g2 in range(4, 8):
                gate_group(g2)
                units(a_out.first, g2, g2 + 1)
                group_low(g2)
            for b in range(1, NB):
                units(a_out.unit(b), 0, RING)
                gain_block(0, b - 1)
                units(a_out.unit(b), RING, U)

            dve.wait_ge(taps_ready, 1)

            def after_normed(s, nxt):
                begin_post_norm(s)
                post_norm(s, 0)
                for c in range(NB):
                    update_stream(s, c, 0)
                units(nxt.first, 0, 1)
                post_norm(s, 1)
                turn_and_split(s + 1, nxt)

            def ffn_taps(layer, i, part, tap, ff_block):
                for m in range(TB):
                    tile = i * TB + (part * FT + m)
                    w = conv_cols[:, layer, tap, bass.ds(tile, 1)]
                    src = conv_in[:, m, tap:tap + T]
                    if tap == PAD:
                        ins = dve.tensor_scalar(conv[:, m, :], src, w, conv_cols[:, layer, TAPS, bass.ds(tile, 1)],
                                                ALU.mult, ALU.add)
                    else:
                        ins = dve.scalar_tensor_tensor(out=conv[:, m, :], in0=src, scalar=w, in1=conv[:, m, :],
                                                       op0=ALU.mult, op1=ALU.add)
                ins.then_inc(conv_step, 1)

            def ffn_block(layer, i, part, base, a, e):
                ff = i * 2 + (2 * FP * layer + part)
                low_no = i * 2 + (2 * FP * layer + part + NB + 2 * NB * layer + 1)
                add_low(conv_in[:, :, PAD:PAD + T], low_no, column_bank(part))
                scale_tokens(conv_in[:, :, PAD:PAD + T], i * 2 + (UP[layer].block0 + part), low_no)
                units(base, a + RING, a + RING + 1)
                dve.wait_ge(combined, low_no)
                if part:
                    dve.wait_ge(silu_ready, i + (layer * FP + 1))
                ffn_taps(layer, i, part, 2, ff)
                units(base, a + RING + 1, a + RING + 2)
                dve.wait_ge(conv_step, ff * 3 + 1)
                ffn_taps(layer, i, part, 1, ff)
                units(base, a + RING + 2, a + RING + 3)
                dve.wait_ge(conv_step, ff * 3 + 2)
                ffn_taps(layer, i, part, 0, ff)
                if part:
                    dve.wait_ge(conv_step, ff * 3 + 3)
                    dve.tensor_tensor(conv[:, :, :], conv[:, :, :], silu[:, :, :], ALU.mult).then_inc(gated, 1)
                units(base, a + RING + 3, e)
                if part:
                    dve.wait_ge(g_hi_ready, i + (layer * FP + 1))
                    dve.tensor_tensor(g_parts[:, bass.ds(i * TB, TB), LO, :], conv[:, :, :],
                                      g_parts[:, bass.ds(i * TB, TB), HI, :].bitcast(F32), ALU.subtract
                                      ).then_inc(g_ready, 1)

            def ffn_up(layer, s):
                ph = UP[layer]
                after_normed(s, ph)
                units(ph.first, U, U + 3)
                copy_row_scale(s + 1)
                units(ph.first, U + 3, U + RING)
                ffn_block(layer, 0, 0, ph.first, U, 2 * U)
                with dve.Fori(1, ph.pairs) as i:
                    base = i * (2 * U) + ph.first
                    units(base, 0, RING)
                    ffn_block(layer, i - 1, 1, base, 0, U)
                    units(base, U, U + RING)
                    ffn_block(layer, i, 0, base, U, 2 * U)

            def ffn_down(layer, s):
                ph = DOWN[layer]
                units(ph.first, 0, RING)
                ffn_block(layer, FP - 1, 1, ph.first, 0, U)
                units(ph.first, U, ph.units)
                for b in range(1, NB):
                    k = b * ph.units
                    units(ph.first, k, k + RING)
                    gain_block(s, b - 1)
                    units(ph.first, k + RING, k + ph.units)

            ffn_up(0, 0)
            ffn_down(0, 1)

            after_normed(1, q_in)
            low_no = NB + 2 * FP
            for ph in (q_in, k_in):
                for b in range(NB):
                    if ph is q_in and b == 0:
                        continue
                    units(ph.unit(b), 0, 3)
                    if low_no == NB + 2 * FP:
                        copy_row_scale(2)
                    units(ph.unit(b), 3, RING)
                    low_no += 1
                    to, c = (q_t, (b - 1) % NB) if (ph is q_in or b == 0) else (k_t, b - 1)
                    to_block = to[:, c * TB:(c + 1) * TB, :]
                    add_low(to_block, low_no, column_bank((b + 1) % 2), SCALE if to is q_t else None)
                    scale_tokens(to_block, ph.block0 + b - 1, low_no)
                    units(ph.unit(b), RING, U)
                    if ph is q_in:
                        kv_low(kv_tiles(b))

            def att_softplus(j):
                dve.wait_ge(att_act, 4 * j + 3)
                if j:
                    dve.wait_ge(summed, j)
                dve.scalar_tensor_tensor(out=att_sp[:, :, :], in0=ps[:, 4:6, 0:ATT], scalar=0.0, in1=att_log[:, :, :],
                                         op0=ALU.max, op1=ALU.add).then_inc(att_dve, 1)
                dve.wait_ge(att_dve, 4 * j + 1)
                for c in (0, T):
                    last = dve.tensor_tensor(att_sp[:, :, c:c + P], att_sp[:, :, c:c + P],
                                             mask[:, :].unsqueeze(1).to_broadcast([P, 2, P]), ALU.mult)
                last.then_inc(att_dve, 1)
                dve.scalar_tensor_tensor(out=log_beta[:, :, :], in0=ps[:, 4:6, 0:ATT], scalar=0.0,
                                         in1=att_log[:, :, :], op0=ALU.min, op1=ALU.subtract).then_inc(att_dve, 1)

            def att_split(j):
                dve.wait_ge(att_act, 4 * j + 4)
                dve.tensor_tensor(sp_lo[:, :, :], att_sp[:, :, :], sp_hi[:, :, :].bitcast(F32), ALU.subtract
                                  ).then_inc(att_dve, 1)

            def att_exponent(j):
                dve.wait_ge(summed, j + 1)
                dve.wait_ge(att_dve, 4 * j + 3)
                if j:
                    dve.wait_ge(weights_ready, j)
                dve.tensor_tensor(att_exp[:, :, 0:T], log_beta[:, :, 0:T],
                                  ps[:, 6, :].rearrange("p (a t) -> p a t", a=2), ALU.subtract)
                dve.tensor_tensor(att_exp[:, :, T:ATT], log_beta[:, :, T:ATT],
                                  ps[:, 7, 0:T].rearrange("p (a t) -> p a t", a=2), ALU.subtract
                                  ).then_inc(exponent_ready, 1)

            def out_low(j):
                dve.wait_ge(o_hi_ready, j + 1)
                dve.tensor_tensor(o_parts[:, 2 * j:2 * j + 2, LO, :],
                                  ps[:, weighted_bank(j), :].rearrange("p (a t) -> p a t", a=2),
                                  o_parts[:, 2 * j:2 * j + 2, HI, :].bitcast(F32), ALU.subtract).then_inc(o_ready, 1)

            for n in range(V_UNITS + b_out.units):
                units(v_in.first, n, n + 1)
                if n == RING - 1:
                    add_low(k_t[:, LAST * TB:(LAST + 1) * TB, :], low_no + 1, column_bank(1))
                    scale_tokens(k_t[:, LAST * TB:(LAST + 1) * TB, :], k_in.block_end - 1, low_no + 1)
                j = step_at(n, WEIGHTS)
                if j is not None:
                    att_exponent(j)
                j = step_at(n, SOFTPLUS)
                if j is not None:
                    att_softplus(j)
                j = step_at(n, SPLIT)
                if j is not None:
                    att_split(j)
                for j in range(STEPS):
                    if n == OUT_SLOT[j]:
                        out_low(j)
            for b in range(1, NB):
                units(b_out.unit(b), 0, RING)
                gain_block(2, b - 1)
                units(b_out.unit(b), RING, U)

            ffn_up(1, 2)
            ffn_down(1, 3)
            begin_post_norm(3)
            post_norm(3, 0)
            for c in range(NB):
                update_stream(3, c, 0)
            post_norm(3, 1)
            for c in range(NB):
                update_stream(3, c, 1)

        @block.tensor
        def _(pe):
            U = gate_v.units

            def columns_out(ph, i, src, ready, first_ready, flip=0, t=None):
                for hb in range(2):
                    bank = column_bank(hb, flip)
                    for u in range(ph.units):
                        k = hb * ph.units + u
                        slot = k % RING
                        pe.wait_ge(unit_split, i * (2 * ph.units) + (ph.first + k + 1))
                        pe.wait_ge(ready, first_ready + UK * u + UK)
                        if u == 0:
                            pe.wait_ge(evacuated, i * 2 + (ph.block0 + hb - 1))
                            if t is not None and hb:
                                pe.wait_ge(row_ready, t + 1)
                        for m in range(TB):
                            for kk in range(UK):
                                kt = UK * u + kk
                                first, last = kt == 0, kt == KT - 1
                                pe.matmul(ps[:, bank + m, :], w_hi[:, slot, kk, m * P:(m + 1) * P],
                                          src[:, kt, :, :].rearrange("p a t -> p (a t)"), start=first, stop=False,
                                          skip_group_check=True)
                                mm = pe.matmul(ps[:, bank + m, 0:T], w_lo[:, slot, kk, m * P:(m + 1) * P],
                                               src[:, kt, HI, :], start=False, stop=last, skip_group_check=True)
                        mm.then_inc(unit_used, 1)
                        if t is not None and hb == 0:
                            turn_rest(t, u)

            def tokens_out_half(ph, hb, u, half, src, bank):
                slot = (hb * ph.units + u) % RING
                t0 = half * P
                for kk in range(UK):
                    kt = UK * u + kk
                    first, last = kt == 0, kt == UK * ph.units - 1
                    to = ps[:, bank + half, :]
                    pe.matmul(to, src[:, kt, HI, t0:t0 + P], w_hi[:, slot, kk, :], start=first, stop=False)
                    pe.matmul(to, src[:, kt, HI, t0:t0 + P], w_lo[:, slot, kk, :], start=False, stop=False)
                    mm = pe.matmul(to, src[:, kt, LO, t0:t0 + P], w_hi[:, slot, kk, :], start=False, stop=last)
                return mm

            def tokens_out_unit(ph, hb, u, src, bank):
                tokens_out_half(ph, hb, u, 0, src, bank)
                tokens_out_half(ph, hb, u, 1, src, bank).then_inc(unit_used, 1)

            def last_units(ph, i, hb, src, ready, count, bank):
                for u in range(ph.units - RING, ph.units):
                    pe.wait_ge(unit_split, i * (2 * ph.units) + (ph.first + hb * ph.units + u + 1))
                    pe.wait_ge(ready, count(u))
                    mm = tokens_out_half(ph, hb, u, 0, src, bank)
                mm.then_inc(half_done, 1)
                for u in range(ph.units - RING, ph.units):
                    tokens_out_half(ph, hb, u, 1, src, bank).then_inc(unit_used, 1)

            def tokens_out(ph, i, src, ready, count, t=None):
                for hb in range(2):
                    tokens_out_block(ph, i, hb, src, ready, count, t if hb == 0 else None)

            def tokens_out_block(ph, i, hb, src, ready, count, t=None):
                bank = token_bank(ph, hb)
                for u in range(ph.units - RING if ph in NORMED else ph.units):
                    pe.wait_ge(unit_split, i * (2 * ph.units) + (ph.first + hb * ph.units + u + 1))
                    pe.wait_ge(ready, count(u))
                    if u == 0 and not (ph is gate_v and isinstance(i, int) and i == 0):
                        pe.wait_ge(evacuated, i * 2 + (ph.block0 + hb - 1))
                    tokens_out_unit(ph, hb, u, src, bank)
                    if t is not None:
                        turn_rest(t, u)
                if ph in NORMED:
                    last_units(ph, i, hb, src, ready, count, bank)

            def turn(t, tiles):
                for k in tiles:
                    if k % TB == 0:
                        if t:
                            for half in range(NH):
                                pe.wait_ge(h_new[half], NB * (t - 1) + k // TB + 1)
                        else:
                            pe.wait_ge(x_loaded[k // TB], 16)
                    if k >= 4:
                        if t == KV_NORM:
                            pe.wait_ge(kv_kept, k - 4 + 1)
                        else:
                            pe.wait_ge(x_ready, KT * t + k - 4 + 1)
                    for half in range(NH):
                        tr = pe.transpose(turned(k)[:, half * P:(half + 1) * P], h[:, half, k * P:(k + 1) * P],
                                          ident[:, :])
                    tr.then_inc(x_turned, 1)

            def turn_rest(t, u):
                if u == 0:
                    turn(t, range(4, 8))
                if u == 1:
                    turn(t, range(8, 12))
                if u == 3:
                    turn(t, range(12, KT))
                if u == 6:
                    if t == KV_NORM:
                        pe.wait_ge(kv_kept, KT - 3)
                    pe.wait_ge(diag_ready, t + 1)
                    for half in range(NH):
                        mm = pe.matmul(ps[:, 4, half * P:(half + 1) * P], ones[:, :], diag[:, half, :],
                                       start=True, stop=True)
                    mm.then_inc(row_spread, 1)

            pe.wait_ge(constants, 8)
            pe.wait_ge(mix_gains_loaded, 16)
            pe.transpose(ps[:, 3, 0:2 * KT], gain_rows[0:2 * KT, :], ident[0:2 * KT, 0:2 * KT]).then_inc(gains_turned, 1)
            turn(0, range(0, 4))
            pe.wait_ge(gains_ready, 1)
            tokens_out(gate_v, 0, x_parts, x_ready, lambda u: UK * u + UK, t=0)
            pe.wait_ge(spatial_masked, 1)
            pe.wait_ge(row_ready, 1)
            for g in range(G):
                tr = pe.transpose(ps[:, 4 + g // 4, (g % 4) * P:(g % 4 + 1) * P], ws_nat[:, g, :], ident[:, :])
            tr.then_inc(spatial_turned, 1)
            for hb in range(2):
                tokens_out_block(gate_v, 1, hb, x_parts, x_ready, lambda u: UK * u + UK)
                if hb == 0:
                    pe.wait_ge(ws_ready, 1)
                    pe.wait_ge(taps_loaded, 16 * 4)
                    for row in range(2 * (TAPS + 1)):
                        c = (row % (TAPS + 1)) * 2 * FT
                        pe.transpose(ps[:, 4 + row // (TAPS + 1), c:c + 2 * FT], conv_rows[0:2 * FT, row, :],
                                     ident[0:2 * FT, 0:2 * FT])
                    pe.wait_ge(gains_loaded, 16 * 2)
                    tr = pe.transpose(ps[:, 6, 0:NGAIN], gain_rows[0:NGAIN, :], ident[0:NGAIN, 0:NGAIN])
                    tr.then_inc(taps_turned, 1)
            pe.wait_ge(taps_ready, 1)
            with pe.Fori(0, gate_u.pairs) as i:
                columns_out(gate_u, i, x_parts, x_ready, 0, flip=1)

            pe.wait_ge(v_normed, NH)
            pe.wait_ge(bias_ready, 16)
            pe.wait_ge(evacuated, gate_u.block_end - 1)
            for g2 in range(G // 2):
                if g2 == 4:
                    pe.wait_ge(evacuated, gate_u.block_end)
                bank = mixing_bank(g2)
                bias = bias_parts[:, 2 * g2:2 * g2 + 2, :].unsqueeze(2).to_broadcast([2, 2, NH, P])
                pe.matmul(ps[:, bank, :].rearrange("p (g a t) -> p g a t", g=2, a=NH), ones_r[0:2, :], bias,
                          start=True, stop=False, skip_group_check=True)
                for j in range(4):
                    g, chunk = 2 * g2 + j // 2, j % 2
                    mm = pe.matmul(ps[:, bank, j * P:(j + 1) * P], v_nat[:, chunk, g, :], ws_t[:, g, :],
                                   start=False, stop=(j == 3), skip_group_check=True)
                mm.then_inc(group_mixed, 1)
            pe.wait_ge(group_gated, 4)
            with pe.Fori(0, a_out.pairs) as i:
                tokens_out(a_out, i, mix_parts, group_ready, lambda u: u + 1)

            for layer in range(2):
                t = 1 + 2 * layer
                turn(t, range(0, 4))
                columns_out(UP[layer], 0, x_parts, x_ready, KT * t, t=t)
                with pe.Fori(1, FP) as i:
                    columns_out(UP[layer], i, x_parts, x_ready, KT * t)
                with pe.Fori(0, DOWN[layer].pairs) as i:
                    tokens_out(DOWN[layer], i, g_parts, g_ready, lambda u: layer * FP + (UK * u + 1) // TB + 1)
                if layer == 1:
                    break

                turn(2, range(0, 4))
                columns_out(q_in, 0, x_parts, x_ready, KT * 2, t=2)
                with pe.Fori(1, q_in.pairs) as i:
                    columns_out(q_in, i, x_parts, x_ready, KT * 2)
                with pe.Fori(0, k_in.pairs) as i:
                    columns_out(k_in, i, kv_parts, kv_ready, 0)

                def score(j):
                    pe.wait_ge(combined, NB + 2 * FP + 2 * NB)
                    if j:
                        pe.wait_ge(att_dve, 4 * (j - 1) + 3)
                    for a in range(2):
                        hd = 2 * j + a
                        pe.matmul(ps[:, 4 + a, 0:T], k_t[:, hd, 0:P], q_t[:, hd, :], start=True, stop=True)
                        mm = pe.matmul(ps[:, 4 + a, T:ATT], k_t[:, hd, P:T], q_t[:, hd, P:T], start=True, stop=True)
                    mm.then_inc(scored, 1)

                def sum_later(j):
                    pe.wait_ge(att_dve, 4 * j + 4)
                    if j:
                        pe.wait_ge(exponent_ready, j)
                    early = ps[:, 6, :].rearrange("p (a t) -> p a t", a=2)
                    for part in (sp_hi, sp_lo):
                        pe.matmul(early, later[:, :], part[:, :, 0:T], start=(part is sp_hi), stop=False,
                                  skip_group_check=True)
                        pe.matmul(early[:, :, P:T], ones_r[:, :], part[:, :, T:ATT], start=False,
                                  stop=(part is sp_lo), skip_group_check=True)
                        mm = pe.matmul(ps[:, 7, 0:T].rearrange("p (a t) -> p a t", a=2), later[:, :],
                                       part[:, :, T:ATT], start=(part is sp_hi), stop=(part is sp_lo),
                                       skip_group_check=True)
                    mm.then_inc(summed, 1)

                def weight_values(j):
                    pe.wait_ge(evacuated, v_in.block0 + j // 2 + 1)
                    pe.wait_ge(att_ready, STEPS)
                    if j >= 4:
                        pe.wait_ge(o_ready, j - 3)
                    bank = weighted_bank(j)
                    for a in range(2):
                        hd = 2 * j + a
                        pe.matmul(ps[:, bank, a * T:(a + 1) * T], val[:, 0, hd * P:(hd + 1) * P], att[:, hd, 0:T],
                                  start=True, stop=False, skip_group_check=True)
                        mm = pe.matmul(ps[:, bank, a * T + P:(a + 1) * T], val[:, 1, hd * P:(hd + 1) * P],
                                       att[:, hd, T:ATT], start=False, stop=True, skip_group_check=True)
                    mm.then_inc(weighted, 1)

                for n in range(V_UNITS + b_out.units - RING):
                    b, u = n // U, n % U
                    hb = b % 2
                    pe.wait_ge(unit_split, v_in.first + n + 1)
                    if b < NB:
                        if u == 0:
                            pe.wait_ge(evacuated, v_in.block0 + b - 1)
                        tokens_out_unit(v_in, hb, u, kv_parts, token_bank(v_in, hb))
                    else:
                        pe.wait_ge(o_ready, u + 1)
                        if u == 0:
                            pe.wait_ge(evacuated, b_out.block0 - 1)
                        tokens_out_unit(b_out, 0, u, o_parts, token_bank(b_out, 0))
                    j = step_at(n, SUMS)
                    if j is not None:
                        sum_later(j)
                    j = step_at(n, SCORES)
                    if j is not None:
                        score(j)
                    for j in range(STEPS):
                        if n == WEIGHTED[j]:
                            weight_values(j)
                last_units(b_out, 0, 0, o_parts, o_ready, lambda u: u + 1, token_bank(b_out, 0))
                tokens_out_block(b_out, 0, 1, o_parts, o_ready, lambda u: u + 1)
                with pe.Fori(1, b_out.pairs) as i:
                    tokens_out(b_out, i, o_parts, o_ready, lambda u: u + 1)


_INS = ['x', 'pre_mix_g', 'post_mix_g', 'pre_ffn_g', 'post_ffn_g', 'a_w_in', 'a_v_norm_g', 'a_w_spatial',
        'a_b_spatial', 'a_w_out', 'kv_norm_g', 'w_k', 'w_v', 'b_w_q', 'b_w_o', 'ffn_w_up', 'ffn_conv_w',
        'ffn_conv_b', 'ffn_w_down']


def kernel(**inputs):
    import numpy as np
    import concourse.bacc as bacc
    from concourse.bass_utils import run_bass_kernel_spmd

    nc = bacc.Bacc("TRN2", target_bir_lowering=False, num_devices=1)
    arrays, args = {}, []
    for name in _INS:
        a = np.ascontiguousarray(inputs[name])
        arrays[f"in_{name}"] = a
        args.append(nc.dram_tensor(f"in_{name}", a.shape, mybir.dt.from_np(a.dtype), kind="ExternalInput").ap())
    args.append(nc.dram_tensor("out", arrays["in_x"].shape, F32, kind="ExternalOutput").ap())
    build_trunk(nc, *args)
    r = run_bass_kernel_spmd(nc, [arrays], core_ids=[0])
    return r.results[0]["out"]
```
